# Optimizing a Trainium2 kernel written in Bass

```python
import jax, jax.numpy as jnp
from jax import lax
import numpy as np

D_MODEL = 2048
BATCH = 1
SEQ = 256
DEPTH = 1

HEAD_DIM = 128
RET_HEADS = (D_MODEL // 2) // HEAD_DIM
ATT_Q_HEADS = (D_MODEL // 2) // HEAD_DIM
ATT_KV_HEADS = ATT_Q_HEADS // 4
RET_WIDTH = RET_HEADS * HEAD_DIM
ATT_WIDTH = ATT_Q_HEADS * HEAD_DIM
KV_WIDTH = ATT_KV_HEADS * HEAD_DIM
MIX_WIDTH = RET_WIDTH + ATT_WIDTH
IN_WIDTH = 4 * RET_WIDTH + ATT_WIDTH + 2 * KV_WIDTH
D_FF = 256 * ((8 * D_MODEL // 3 + 255) // 256)
CHUNK = 128
WINDOW = 128
ROPE_THETA = 500000.0
ROPE_DIM = HEAD_DIM // 4
RET_THETA = 10000.0
EPS = 1e-6

kernel_name = "hybrid_retention_swa_sink_macaron"

def rms_norm(x, g):
    xf = x.astype(jnp.float32)
    y = xf * lax.rsqrt(jnp.mean(xf * xf, axis=-1, keepdims=True) + EPS)
    return (y * g.astype(jnp.float32)).astype(x.dtype)

def rope_tables(seq_len, dim, theta):
    inv = theta ** (-jnp.arange(0, dim, 2, dtype=jnp.float32) / dim)
    ang = jnp.arange(seq_len, dtype=jnp.float32)[:, None] * inv[None, :]
    ang = jnp.concatenate([ang, ang], axis=-1)
    return jnp.cos(ang), jnp.sin(ang)

def apply_rotary(x, cos, sin):
    c = cos[None, :, None, :].astype(x.dtype)
    s = sin[None, :, None, :].astype(x.dtype)
    x1, x2 = jnp.split(x, 2, axis=-1)
    return x * c + jnp.concatenate([-x2, x1], axis=-1) * s

def swiglu(h, w_gate, w_up, w_down):
    return (jax.nn.silu(h @ w_gate) * (h @ w_up)) @ w_down

def retention(q, k, v):
    B, S, H, d = q.shape
    dv = v.shape[-1]
    nc = S // CHUNK
    q = q.astype(jnp.float32)
    k = k.astype(jnp.float32) * (d ** -0.5)
    v = v.astype(jnp.float32)
    log_g = jnp.log1p(-jnp.exp2(-5.0 - jnp.arange(H, dtype=jnp.float32)))
    pos = jnp.arange(CHUNK, dtype=jnp.float32)
    diff = pos[:, None] - pos[None, :]
    intra_decay = jnp.where(diff[None] >= 0,
                            jnp.exp(jnp.maximum(diff, 0.0)[None] * log_g[:, None, None]), 0.0)
    qc = q.reshape(B, nc, CHUNK, H, d)
    kc = k.reshape(B, nc, CHUNK, H, d)
    vc = v.reshape(B, nc, CHUNK, H, dv)
    scores = jnp.einsum('bcnhd,bcmhd->bchnm', qc, kc) * intra_decay
    intra = jnp.einsum('bchnm,bcmhe->bcnhe', scores, vc)
    k_tail = jnp.exp((CHUNK - 1.0 - pos)[:, None] * log_g[None, :])
    chunk_kv = jnp.einsum('bcmhd,bcmhe->bchde', kc * k_tail[:, :, None], vc)
    chunk_decay = jnp.exp(CHUNK * log_g)[None, :, None, None]

    def step(state, kv):
        return state * chunk_decay + kv, state

    _, prev = lax.scan(step, jnp.zeros((B, H, d, dv), jnp.float32), jnp.moveaxis(chunk_kv, 1, 0))
    prev = jnp.moveaxis(prev, 0, 1)
    q_head = jnp.exp((pos + 1.0)[:, None] * log_g[None, :])
    cross = jnp.einsum('bcnhd,bchde->bcnhe', qc * q_head[:, :, None], prev)
    return (intra + cross).reshape(B, S, H, dv)

def sliding_window_sink_attention(q, k, v, sinks):
    B, S, Hq, d = q.shape
    Hkv = k.shape[2]
    G = Hq // Hkv
    nb = S // WINDOW
    qb = q.reshape(B, nb, WINDOW, Hkv, G, d)
    kb = k.reshape(B, nb, WINDOW, Hkv, d)
    vb = v.reshape(B, nb, WINDOW, Hkv, d)
    shift = lambda t: jnp.concatenate([jnp.zeros_like(t[:, :1]), t[:, :-1]], axis=1)
    kk = jnp.concatenate([shift(kb), kb], axis=2)
    vv = jnp.concatenate([shift(vb), vb], axis=2)
    s = jnp.einsum('bnqhgd,bnkhd->bnhgqk', qb, kk).astype(jnp.float32) * (d ** -0.5)
    blk = jnp.arange(nb)[:, None, None]
    qi = jnp.arange(WINDOW)[None, :, None]
    kj = jnp.arange(2 * WINDOW)[None, None, :]
    rel = WINDOW + qi - kj
    kpos = (blk - 1) * WINDOW + kj
    mask = (rel >= 0) & (rel < WINDOW) & (kpos >= 0)
    s = jnp.where(mask[None, :, None, None], s, jnp.finfo(jnp.float32).min)
    sink_col = jnp.broadcast_to(sinks.astype(jnp.float32).reshape(1, 1, Hkv, G, 1, 1),
                                s.shape[:-1] + (1,))
    p = jax.nn.softmax(jnp.concatenate([s, sink_col], axis=-1), axis=-1)[..., :-1]
    o = jnp.einsum('bnhgqk,bnkhd->bnqhgd', p.astype(v.dtype), vv)
    return o.reshape(B, S, Hq * d)

def setup_inputs(seed: int = 0) -> dict:
    key = jax.random.key(seed)
    ks = jax.random.split(key, 16)
    f32 = jnp.float32
    nrm = lambda k, shape, scale: jax.random.normal(k, shape, f32) * scale
    gain = lambda k, shape: 1.0 + 0.02 * jax.random.normal(k, shape, f32)
    return {
        "x": jax.random.normal(ks[0], (BATCH, SEQ, D_MODEL), f32),
        "ffn1_norm": gain(ks[1], (DEPTH, D_MODEL)),
        "ffn1_w_gate": nrm(ks[2], (DEPTH, D_MODEL, D_FF), D_MODEL ** -0.5),
        "ffn1_w_up": nrm(ks[3], (DEPTH, D_MODEL, D_FF), D_MODEL ** -0.5),
        "ffn1_w_down": nrm(ks[4], (DEPTH, D_FF, D_MODEL), D_FF ** -0.5),
        "mix_norm": gain(ks[5], (DEPTH, D_MODEL)),
        "w_in": nrm(ks[6], (DEPTH, D_MODEL, IN_WIDTH), D_MODEL ** -0.5),
        "q_norm": gain(ks[7], (DEPTH, HEAD_DIM)),
        "k_norm": gain(ks[8], (DEPTH, HEAD_DIM)),
        "attn_sinks": nrm(ks[9], (DEPTH, ATT_Q_HEADS), 1.0),
        "w_out": nrm(ks[10], (DEPTH, MIX_WIDTH, D_MODEL), MIX_WIDTH ** -0.5),
        "ffn2_norm": gain(ks[11], (DEPTH, D_MODEL)),
        "ffn2_w_gate": nrm(ks[12], (DEPTH, D_MODEL, D_FF), D_MODEL ** -0.5),
        "ffn2_w_up": nrm(ks[13], (DEPTH, D_MODEL, D_FF), D_MODEL ** -0.5),
        "ffn2_w_down": nrm(ks[14], (DEPTH, D_FF, D_MODEL), D_FF ** -0.5),
    }

def reference(x, ffn1_norm, ffn1_w_gate, ffn1_w_up, ffn1_w_down, mix_norm, w_in, q_norm, k_norm,
              attn_sinks, w_out, ffn2_norm, ffn2_w_gate, ffn2_w_up, ffn2_w_down):
    B, S, _ = x.shape
    cos_a, sin_a = rope_tables(S, ROPE_DIM, ROPE_THETA)
    cos_r, sin_r = rope_tables(S, HEAD_DIM, RET_THETA)
    split_at = [RET_WIDTH, 2 * RET_WIDTH, 3 * RET_WIDTH, 4 * RET_WIDTH,
                4 * RET_WIDTH + ATT_WIDTH, 4 * RET_WIDTH + ATT_WIDTH + KV_WIDTH]
    for l in range(DEPTH):
        h = rms_norm(x, ffn1_norm[l])
        x = x + 0.5 * swiglu(h, ffn1_w_gate[l], ffn1_w_up[l], ffn1_w_down[l])

        h = rms_norm(x, mix_norm[l])
        z = h @ w_in[l]
        q_r, k_r, v_r, g_r, q_a, k_a, v_a = jnp.split(z, split_at, axis=-1)

        q_r = apply_rotary(q_r.reshape(B, S, RET_HEADS, HEAD_DIM), cos_r, sin_r)
        k_r = apply_rotary(k_r.reshape(B, S, RET_HEADS, HEAD_DIM), cos_r, sin_r)
        v_r = v_r.reshape(B, S, RET_HEADS, HEAD_DIM)
        y_r = retention(q_r, k_r, v_r)
        y_r = y_r * lax.rsqrt(jnp.mean(y_r * y_r, axis=-1, keepdims=True) + EPS)
        y_r = (jax.nn.silu(g_r.astype(jnp.float32)) * y_r.reshape(B, S, RET_WIDTH)).astype(x.dtype)

        q_a = rms_norm(q_a.reshape(B, S, ATT_Q_HEADS, HEAD_DIM), q_norm[l])
        k_a = rms_norm(k_a.reshape(B, S, ATT_KV_HEADS, HEAD_DIM), k_norm[l])
        q_a = jnp.concatenate([apply_rotary(q_a[..., :ROPE_DIM], cos_a, sin_a), q_a[..., ROPE_DIM:]], axis=-1)
        k_a = jnp.concatenate([apply_rotary(k_a[..., :ROPE_DIM], cos_a, sin_a), k_a[..., ROPE_DIM:]], axis=-1)
        v_a = v_a.reshape(B, S, ATT_KV_HEADS, HEAD_DIM)
        y_a = sliding_window_sink_attention(q_a, k_a, v_a, attn_sinks[l])

        x = x + jnp.concatenate([y_r, y_a.astype(x.dtype)], axis=-1) @ w_out[l]

        h = rms_norm(x, ffn2_norm[l])
        x = x + 0.5 * swiglu(h, ffn2_w_gate[l], ffn2_w_up[l], ffn2_w_down[l])
    return x


_drawn_inputs = setup_inputs


def setup_inputs(seed=0):
    import zlib

    import numpy as np

    out = dict(_drawn_inputs(seed))
    spreads = {}
    factors = {'ffn1_norm': 5.308,
     'mix_norm': 3.346,
     'q_norm': 8.0,
     'k_norm': 8.0,
     'attn_sinks': 95.372,
     'ffn2_norm': 7.962}
    for name, (base, spread) in spreads.items():
        noise = np.random.default_rng([zlib.crc32(name.encode()), seed]).standard_normal(out[name].shape)
        drawn = base * np.exp(spread * noise) if base else spread * noise
        out[name] = __import__('jax').numpy.asarray(drawn.astype(out[name].dtype))
    for name, factor in factors.items():
        out[name] = (out[name] * factor).astype(out[name].dtype)
    return out
```

```python
from contextlib import ExitStack

import concourse.bass as bass
from concourse import mybir

F32 = mybir.dt.float32
F32R = mybir.dt.float32r
ACT = mybir.ActivationFunctionType
ALU = mybir.AluOpType
AX_X = mybir.AxisListType.X

P = 128
EPS = 1e-6
NEG = -1e30

D_MODEL = 2048
SEQ = 256
D_FF = 5632
HD = 128
ROPE = 32
NTOK = SEQ // P
UW = 512
KT = UW // P
KG = D_MODEL // UW
NG = D_MODEL // UW
CH = D_FF // UW
HEADS = UW // HD
RAW = 4
SPLIT = 3
LEAD = SPLIT - 1

MIX = [("in", "kv", 5120), ("in", "qa0", 4096), ("in", "qa1", 4608),
       ("in", "qr0", 0), ("in", "kr0", 1024), ("in", "vr0", 2048), ("out", "a0", 1024),
       ("in", "gr0", 3072), ("in", "qr1", 512), ("in", "kr1", 1536), ("out", "a1", 1536),
       ("in", "vr1", 2560), ("in", "gr1", 3584), ("out", "r0", 0), ("out", "r1", 512)]
CHUNK_OF = {name: s for s, (_, name, _) in enumerate(MIX)}
OUTS = [name for kind, name, _ in MIX if kind == "out"]

FFN_UNITS = CH * (2 * KG + NG)
MIX_UNITS = 4 * len(MIX)
FIRST = {"ffn1": 0, "mix": FFN_UNITS, "ffn2": FFN_UNITS + MIX_UNITS}
UNITS = 2 * FFN_UNITS + MIX_UNITS

WORK = ["T ka", "T qa0", "S1 a0", "S0 a0", "PT1 a0", "PT0 a0", "PV a0", "T qa1", "S1 a1", "S0 a1",
        "T qr0", "PT1 a1", "PT0 a1", "PV a1", "T kr0", "R1 r0", "R0 r0", "Y r0", "TY r0",
        "T qr1", "T kr1", "R1 r1", "R0 r1", "Y r1", "TY r1"]
ROWS = ["ka", "qa0", "P1 a0", "P0 a0", "qa1", "qr0", "P1 a1", "P0 a1", "kr0", "y r0", "qr1", "kr1", "y r1"]
STATS = ["ka", "qa0", "qa1", "y r0", "y r1"]
Z_VECTOR = ["kv", "qa0", "qa1", "qr0", "kr0", "qr1", "kr1"]
Z_SCALAR = ["vr0", "gr0", "vr1", "gr1"]
AFTER = {3: ["ka"], 5: ["T ka"], 7: ["qa0"], 9: ["T qa0"], 10: ["S1 a0"], 11: ["S0 a0"],
         13: ["PT1 a0", "qa1"], 14: ["PT0 a0"], 15: ["PV a0", "qr0"], 16: ["T qa1"], 17: ["S1 a1"],
         18: ["S0 a1"], 19: ["T qr0", "kr0"], 20: ["PT1 a1"], 21: ["PT0 a1"], 22: ["PV a1"],
         23: ["T kr0", "vr0"], 24: ["R1 r0"], 25: ["R0 r0"], 26: ["Y r0"], 31: ["gr0"], 33: ["TY r0"],
         35: ["qr1"], 37: ["T qr1"], 39: ["kr1"], 41: ["T kr1"], 42: ["R1 r1"], 43: ["R0 r1"],
         47: ["vr1"], 48: ["Y r1"], 51: ["gr1"], 53: ["TY r1"]}

C_ID, C_COS, C_SIN, C_COSA, C_SINA, C_MASK = 0, 128, 384, 640, 704, 768
C_ALL = 1024


def build(nc, x, gains, ffn, w_in, w_out, q_norm, k_norm, sinks, consts, decay, out):
    with ExitStack() as ctx:
        def sb(name, shape, dt=F32):
            return ctx.enter_context(nc.sbuf_tensor(name, shape, dt))

        def sem(name):
            return ctx.enter_context(nc.semaphore(name))

        raw = sb("raw", [P, RAW, KT, UW])
        w_hi = sb("w_hi", [P, SPLIT, KT, UW], F32R)
        w_lo = sb("w_lo", [P, SPLIT, KT, UW], F32R)
        xs = sb("xs", [P, NTOK, D_MODEL])
        hT_hi = sb("hT_hi", [P, KG, KT * SEQ], F32R)
        hT_lo = sb("hT_lo", [P, KG, KT * SEQ], F32R)
        aT_hi = sb("aT_hi", [P, 2, KT * SEQ], F32R)
        aT_lo = sb("aT_lo", [P, 2, KT * SEQ], F32R)
        gate_s = sb("gate_s", [P, NTOK * UW])
        act_s = sb("act_s", [P, NTOK * UW])
        table = sb("table", [P, D_MODEL])
        rows = sb("rows", [P, 2, NTOK * UW])
        square = sb("square", [P, NTOK * UW])
        kaT = sb("kaT", [P, 2, SEQ])
        qT = sb("qT", [P, HEADS, SEQ])
        krT = sb("krT", [P, HEADS, SEQ])
        s1 = sb("s1", [P, HEADS, SEQ])
        s0 = sb("s0", [P, HEADS, P])
        t1 = sb("t1", [P, 2 * HEADS, P])
        t0 = sb("t0", [P, HEADS, P])
        va = sb("va", [P, NTOK, 2 * HD])
        vr = sb("vr", [P, NTOK, UW])
        const = sb("const", [P, C_ALL])
        qgain = sb("qgain", [P, HD])
        kgain = sb("kgain", [P, HD])
        sink = sb("sink", [P, 2 * HEADS])
        ssq = sb("ssq", [P, NTOK, NG])
        nst = sb("nst", [P, 4 * NTOK])
        hst = sb("hst", [P, 4, 2 * HEADS])
        sst = sb("sst", [P, 8, HEADS])

        spare = sb("spare", [P, 4])

        banks = ctx.enter_context(nc.psum_tensor("banks", [P, 8, UW], F32))

        x_landed = [sem(f"x_landed{n}") for n in range(NG)]
        table_landed = sem("table_landed")
        const_landed = sem("const_landed")
        raw_landed = [sem(f"raw_landed{s}") for s in range(RAW)]
        hi_done = sem("hi_done")
        lo_done = sem("lo_done")
        unit_done = sem("unit_done")
        squared = sem("squared")
        mean_ready = sem("mean_ready")
        root_ready = sem("root_ready")
        normed = sem("normed")
        hT_raw = sem("hT_raw")
        hT_hi_done = sem("hT_hi_done")
        hT_lo_done = sem("hT_lo_done")
        silu_done = sem("silu_done")
        act_ready = sem("act_ready")
        aT_raw = sem("aT_raw")
        aT_hi_done = sem("aT_hi_done")
        aT_lo_done = sem("aT_lo_done")
        mT_hi_done = sem("mT_hi_done")
        half_done = sem("half_done")
        sum_room = sem("sum_room")
        z_free_v = sem("z_free_v")
        z_free_s = sem("z_free_s")
        work_ready = sem("work_ready")
        work_free = sem("work_free")
        rows_ready = sem("rows_ready")
        head_sq = sem("head_sq")
        head_mean = sem("head_mean")
        head_root = sem("head_root")
        score_max = sem("score_max")
        exp_done = sem("exp_done")
        v_copied = sem("v_copied")
        chain = sem("chain")
        stored = sem("stored")

        ident = const[:, C_ID:C_ID + P]
        cos_r = const[:, C_COS:C_COS + NTOK * HD].rearrange("p (t d) -> p t d", t=NTOK)
        sin_r = const[:, C_SIN:C_SIN + NTOK * HD].rearrange("p (t d) -> p t d", t=NTOK)
        cos_a = const[:, C_COSA:C_COSA + NTOK * ROPE].rearrange("p (t d) -> p t d", t=NTOK)
        sin_a = const[:, C_SINA:C_SINA + NTOK * ROPE].rearrange("p (t d) -> p t d", t=NTOK)
        mask = const[:, C_MASK:C_MASK + SEQ]
        decays = table[:, :].rearrange("p (h n) -> p h n", n=SEQ)

        pair = [banks[:, 0:2, :], banks[:, 2:4, :]]
        sums = banks[:, 4:8, :]
        work = banks[:, 6:8, :].rearrange("p b n -> p (b n)")
        flat = lambda a: a.rearrange("p b n -> p (b n)")

        x_d = x.rearrange("o (t p) n -> p (o t) n", p=P)
        out_d = out.rearrange("o (t p) n -> p (o t) n", p=P)

        def by_columns(w):
            return w.rearrange("o (g k p) (c n) -> (o g) c p k n", k=KT, p=P, n=UW)

        def by_rows(w):
            return w.rearrange("o (c k p) (g n) -> (o c) g p k n", k=KT, p=P, n=UW)

        def base(phase):
            return 0 if phase == "ffn1" else CH

        def sums_before(phase):
            return {"ffn1": 0, "mix": 2 * NG * CH, "ffn2": 2 * NG * (CH + len(OUTS))}[phase]

        def up_to(names, name):
            return names.index(name) + 1

        block = ctx.enter_context(nc.Block())

        @block.sync
        def _(sp):
            for n in range(NG):
                sp.dma_start(xs[:, :, n * UW:(n + 1) * UW], x_d[:, :, n * UW:(n + 1) * UW]).then_inc(x_landed[n], 16)
            sp.dma_start(table[:, :], gains[0][0].partition_broadcast(P)).then_inc(table_landed, 16)
            sp.dma_start(const[:, :], consts).then_inc(const_landed, 16)

            def load(u, slot, src, at=None):
                if at is not None or u >= RAW:
                    sp.wait_ge(lo_done, (u if at is None else at) - RAW + 1)
                sp.dma_start(raw[:, slot, :, :], src).then_inc(raw_landed[slot], 16)

            def load_ffn(phase):
                gate, up, down = ffn[phase]
                gate, up, down = by_columns(gate), by_columns(up), by_rows(down)
                u0 = FIRST[phase]
                for g in range(KG):
                    load(u0 + g, g % RAW, gate[g, 0])
                for g in range(KG):
                    load(u0 + KG + g, g % RAW, up[g, 0])
                if phase == "ffn1":
                    sp.dma_start(qgain[:, :], q_norm[0].partition_broadcast(P)).then_inc(const_landed, 16)
                    sp.dma_start(kgain[:, :], k_norm[0].partition_broadcast(P)).then_inc(const_landed, 16)
                    sp.dma_start(sink[:, :], sinks[0].partition_broadcast(P)).then_inc(const_landed, 16)
                    sp.wait_ge(normed, NTOK * KG)
                    sp.dma_start(table[:, :], gains[1][0].partition_broadcast(P)).then_inc(table_landed, 16)
                with sp.Fori(1, CH) as c:
                    first = u0 + 2 * KG + (c - 1) * 12
                    for g in range(KG):
                        load(None, g % RAW, gate[g, c], first + g)
                    for g in range(KG):
                        load(None, g % RAW, up[g, c], first + KG + g)
                    for g in range(NG):
                        load(None, g % RAW, down[c - 1, g], first + 2 * KG + g)
                for g in range(NG):
                    u = u0 + FFN_UNITS - NG + g
                    load(u, u % RAW, down[CH - 1, g])

            load_ffn("ffn1")
            win, wout = by_columns(w_in), by_rows(w_out)
            for s, (kind, name, at) in enumerate(MIX):
                for g in range(4):
                    u = FIRST["mix"] + 4 * s + g
                    load(u, u % RAW, win[g, at // UW] if kind == "in" else wout[at // UW, g])
                if name == "qa0":
                    sp.wait_ge(normed, 2 * NTOK * KG)
                    sp.dma_start(table[:, :], decay).then_inc(table_landed, 16)
                if name == "r0":
                    sp.wait_ge(work_free, up_to(WORK, "R0 r1"))
                    sp.dma_start(table[:, :], gains[2][0].partition_broadcast(P)).then_inc(table_landed, 16)
            load_ffn("ffn2")
            for g in range(NG):
                sp.wait_ge(sum_room, 4 + sums_before("ffn2") + 2 * NG * (CH - 1) + 2 * (g + 1))
                sp.dma_start(out_d[:, :, g * UW:(g + 1) * UW], xs[:, :, g * UW:(g + 1) * UW]).then_inc(stored, 16)
            sp.wait_ge(stored, 16 * NG)

        @block.tensor
        def _(pe):
            def product(slot, left, t, to, start, stop):
                left_hi, left_lo = left
                for k in range(KT):
                    cols = slice((k * NTOK + t) * P, (k * NTOK + t + 1) * P)
                    for n, (a, b) in enumerate(((left_hi, w_hi), (left_hi, w_lo), (left_lo, w_hi))):
                        last = pe.matmul(to, a[:, cols], b[:, slot, k, :],
                                         start=start and k == 0 and n == 0,
                                         stop=stop and k == KT - 1 and n == 2)
                return last

            def columns(u, slot, g, to):
                pe.wait_ge(lo_done, u + 1)
                left = hT_hi[:, g, :], hT_lo[:, g, :]
                for t in range(NTOK):
                    last = product(slot, left, t, to[:, t, :], g == 0, g == KG - 1)
                last.then_inc(unit_done, 1)

            def transpose(to, of, n):
                for i in range(n):
                    last = pe.transpose(to(i), of(i), ident)
                return last

            def rows_sum(u, slot, which, first_sum, to):
                pe.wait_ge(lo_done, u + 1)
                left = aT_hi[:, which, :], aT_lo[:, which, :]
                pe.wait_ge(sum_room, first_sum + 1)
                product(slot, left, 0, to[0], True, True).then_inc(half_done, 1)
                pe.wait_ge(sum_room, first_sum + 2)
                product(slot, left, 1, to[1], True, True).then_inc(unit_done, 1)

            def norm_transposes(n, g):
                done = n * KG + g
                pe.wait_ge(normed, NTOK * (done + 1))
                if done >= 2:
                    pe.wait_ge(hT_lo_done, done - 1)
                at = lambda i: sums[:, 2 * (g % 2) + i // 4, (i % 4) * P:(i % 4 + 1) * P]
                of = lambda i: rows[:, g % 2, ((i % 2) * KT + i // 2) * P:((i % 2) * KT + i // 2 + 1) * P]
                transpose(at, of, KT * NTOK).then_inc(hT_raw, 1)

            def first_chunk(n, u0, to):
                norm_transposes(n, 0)
                norm_transposes(n, 1)
                for g in range(KG):
                    pe.wait_ge(hT_lo_done, n * KG + g + 1)
                    columns(u0 + g, (u0 + g) % SPLIT, g, to)
                    if g + 2 < KG:
                        norm_transposes(n, g + 2)

            def activation_transposes(phase, c, which=0):
                pe.wait_ge(act_ready, base(phase) + c + 1)
                at = lambda i: flat(pair[1])[:, i * P:(i + 1) * P]
                of = lambda i: act_s[:, ((i % 2) * KT + i // 2) * P:((i % 2) * KT + i // 2 + 1) * P]
                transpose(at, of, KT * NTOK).then_inc(aT_raw, 1)

            def multiply_ffn(phase, n):
                u0 = FIRST[phase]
                if phase == "ffn1":
                    pe.wait_ge(const_landed, 16)
                first_chunk(n, u0, pair[0])
                for g in range(KG):
                    columns(u0 + KG + g, (u0 + KG + g) % SPLIT, g, pair[1])
                with pe.Fori(1, CH) as c:
                    u = u0 + 2 * KG + (c - 1) * 12
                    done = base(phase) + c
                    pe.wait_ge(silu_done, done)
                    for g in range(KG):
                        columns(u + g, (2 * KG + g) % SPLIT, g, pair[0])
                        if g == 1:
                            activation_transposes(phase, c - 1)
                    pe.wait_ge(aT_lo_done, done)
                    for g in range(KG):
                        columns(u + KG + g, (3 * KG + g) % SPLIT, g, pair[1])
                    for g in range(NG):
                        s = sums_before(phase) + 2 * NG * (c - 1) + 2 * g
                        rows_sum(u + 2 * KG + g, (4 * KG + g) % SPLIT, 0, s,
                                 [sums[:, (2 * g) % 4, :], sums[:, (2 * g + 1) % 4, :]])
                activation_transposes(phase, CH - 1)
                pe.wait_ge(aT_lo_done, base(phase) + CH)
                for g in range(NG):
                    u = u0 + FFN_UNITS - NG + g
                    s = sums_before(phase) + 2 * NG * (CH - 1) + 2 * g
                    rows_sum(u, u % SPLIT, 0, s, [sums[:, (2 * g) % 4, :], sums[:, (2 * g + 1) % 4, :]])

            def use(name):
                if WORK.index(name):
                    pe.wait_ge(work_free, WORK.index(name))

            def head_transposes(name, of_buffer, n):
                use("T " + name)
                pe.wait_ge(rows_ready, up_to(ROWS, name))
                at = lambda i: work[:, i * P:(i + 1) * P]
                of = lambda i: rows[:, of_buffer, ((i % 2) * n + i // 2) * P:((i % 2) * n + i // 2 + 1) * P]
                transpose(at, of, n * NTOK).then_inc(work_ready, 1)

            def scores1(a):
                use(f"S1 a{a}")
                for h in range(HEADS):
                    last = pe.matmul(work[:, h * SEQ:(h + 1) * SEQ], qT[:, h, P:SEQ], kaT[:, a, :],
                                     start=True, stop=True)
                last.then_inc(work_ready, 1)

            def scores0(a):
                use(f"S0 a{a}")
                for h in range(HEADS):
                    last = pe.matmul(work[:, h * P:(h + 1) * P], qT[:, h, 0:P], kaT[:, a, 0:P],
                                     start=True, stop=True)
                last.then_inc(work_ready, 1)

            def attend(a):
                use(f"PV a{a}")
                pe.wait_ge(v_copied, 1)
                cols = slice(a * HD, (a + 1) * HD)
                for h in range(HEADS):
                    pe.matmul(work[:, h * SEQ:h * SEQ + P], va[:, 0, cols], t0[:, h, :], start=True, stop=True)
                    pe.matmul(work[:, h * SEQ + P:(h + 1) * SEQ], va[:, 0, cols], t1[:, 2 * h, :],
                              start=True, stop=False)
                    last = pe.matmul(work[:, h * SEQ + P:(h + 1) * SEQ], va[:, 1, cols], t1[:, 2 * h + 1, :],
                                     start=False, stop=True)
                last.then_inc(work_ready, 1)

            def retain1(r):
                use(f"R1 r{r}")
                for h in range(HEADS):
                    last = pe.matmul(work[:, h * SEQ:(h + 1) * SEQ], krT[:, h, 0:P], qT[:, h, :],
                                     start=True, stop=True)
                last.then_inc(work_ready, 1)

            def retain0(r):
                use(f"R0 r{r}")
                for h in range(HEADS):
                    last = pe.matmul(work[:, h * P:(h + 1) * P], krT[:, h, P:SEQ], qT[:, h, P:SEQ],
                                     start=True, stop=True)
                last.then_inc(work_ready, 1)

            def retention_rows(r):
                use(f"Y r{r}")
                pe.wait_ge(z_free_s, up_to(Z_SCALAR, f"vr{r}"))
                for h in range(HEADS):
                    cols = slice(h * HD, (h + 1) * HD)
                    pe.matmul(work[:, h * HD:(h + 1) * HD], t1[:, 2 * h, :], vr[:, 0, cols], start=True, stop=True)
                    y1 = work[:, UW + h * HD:UW + (h + 1) * HD]
                    pe.matmul(y1, t1[:, 2 * h + 1, :], vr[:, 0, cols], start=True, stop=False)
                    last = pe.matmul(y1, t0[:, h, :], vr[:, 1, cols], start=False, stop=True)
                last.then_inc(work_ready, 1)

            def side(what):
                kind, _, name = what.partition(" ")
                if kind == "T":
                    head_transposes(name, {"qr0": 1, "kr1": 1}.get(name, 0), 2 if name == "ka" else HEADS)
                elif kind == "TY":
                    use(what)
                    pe.wait_ge(rows_ready, up_to(ROWS, "y " + name))
                    buf = {"r0": 1, "r1": 0}[name]
                    transpose(lambda i: work[:, i * P:(i + 1) * P],
                              lambda i: rows[:, buf, ((i % 2) * KT + i // 2) * P:((i % 2) * KT + i // 2 + 1) * P],
                              KT * NTOK).then_inc(work_ready, 1)
                elif kind == "S1":
                    scores1(int(name[1]))
                elif kind == "S0":
                    scores0(int(name[1]))
                elif kind == "PT1":
                    use(what)
                    pe.wait_ge(rows_ready, up_to(ROWS, "P1 " + name))
                    transpose(lambda i: work[:, i * P:(i + 1) * P],
                              lambda i: s1[:, i // 2, (i % 2) * P:(i % 2 + 1) * P], 2 * HEADS).then_inc(work_ready, 1)
                elif kind == "PT0":
                    use(what)
                    pe.wait_ge(rows_ready, up_to(ROWS, "P0 " + name))
                    transpose(lambda i: work[:, i * P:(i + 1) * P], lambda i: s0[:, i, :],
                              HEADS).then_inc(work_ready, 1)
                elif kind == "PV":
                    attend(int(name[1]))
                elif kind == "R1":
                    retain1(int(name[1]))
                elif kind == "R0":
                    retain0(int(name[1]))
                elif kind == "Y":
                    retention_rows(int(name[1]))

            def pair_free(s):
                if s < 2:
                    return
                kind, name, _ = MIX[s - 2]
                if kind == "out":
                    pe.wait_ge(sum_room, 4 + sums_before("mix") + 2 * NG * OUTS.index(name) + 6)
                elif name in Z_VECTOR:
                    pe.wait_ge(z_free_v, up_to(Z_VECTOR, name))
                else:
                    pe.wait_ge(z_free_s, up_to(Z_SCALAR, name))

            def multiply_mixer():
                u0 = FIRST["mix"]
                pe.wait_ge(silu_done, CH)
                for s, (kind, name, _) in enumerate(MIX):
                    pair_free(s)
                    if s == 0:
                        norm_transposes(1, 0)
                        norm_transposes(1, 1)
                    if kind == "out":
                        pe.wait_ge(work_free, up_to(WORK, {"a": "PV ", "r": "TY "}[name[0]] + name))
                    for g in range(4):
                        t = 4 * s + g
                        u = u0 + t
                        if kind == "in":
                            if s == 0:
                                pe.wait_ge(hT_lo_done, KG + g + 1)
                            columns(u, u % SPLIT, g, pair[s % 2])
                            if s == 0 and g + 2 < KG:
                                norm_transposes(1, g + 2)
                        else:
                            two = pair[s % 2] if g % 2 == 0 else sums[:, 0:2, :]
                            rows_sum(u, u % SPLIT, {"a0": 0, "a1": 1, "r0": 0, "r1": 1}[name],
                                     sums_before("mix") + 2 * NG * OUTS.index(name) + 2 * g,
                                     [two[:, 0, :], two[:, 1, :]])
                        for what in AFTER.get(t, ()):
                            side(what)

            multiply_ffn("ffn1", 0)
            multiply_mixer()
            multiply_ffn("ffn2", 2)

        @block.scalar
        def _(act):
            def split_hi(u, slot, raw_slot, loads):
                act.wait_ge(raw_landed[raw_slot], 16 * loads)
                act.wait_ge(unit_done, u - SPLIT + 1)
                act.activation(w_hi[:, slot, :, :], raw[:, raw_slot, :, :], ACT.Copy).then_inc(hi_done, 1)

            def split(u):
                if u < UNITS:
                    if u < SPLIT:
                        act.wait_ge(raw_landed[u % RAW], 16)
                        act.activation(w_hi[:, u, :, :], raw[:, u, :, :], ACT.Copy).then_inc(hi_done, 1)
                    else:
                        split_hi(u, u % SPLIT, u % RAW, u // RAW + 1)

            def square_x(n, g):
                for t in range(NTOK):
                    if n or g or t:
                        act.wait_ge(squared, (n * NG + g) * NTOK + t)
                    act.activation(square[:, 0:UW], xs[:, t, g * UW:(g + 1) * UW], ACT.Square,
                                   accum_out=ssq[:, t, g:g + 1]).then_inc(squared, 1)

            def square_final_x(phase, s):
                act.wait_ge(sum_room, 4 + sums_before(phase) + s + 2)
                square_x(1 if phase == "ffn1" else 2, s // 2 % NG)

            def norm(n, early):
                act.wait_ge(mean_ready, n + 1)
                act.activation(nst[:, 4:6], nst[:, 2:4], ACT.Sqrt).then_inc(root_ready, 1)
                for g in range(KG):
                    if g < len(early):
                        split(early[g])
                    act.wait_ge(hT_raw, n * KG + g + 1)
                    act.activation(hT_hi[:, g, :], flat(sums[:, 2 * (g % 2):2 * (g % 2) + 2, :]),
                                   ACT.Copy).then_inc(hT_hi_done, 1)

            def split_activation(phase, c, which=0):
                act.wait_ge(aT_raw, base(phase) + c + 1)
                act.activation(aT_hi[:, which, :], flat(pair[1]), ACT.Copy).then_inc(aT_hi_done, 1)

            def silu(phase, c, u):
                act.wait_ge(unit_done, u + 1)
                if phase == "ffn2" or not isinstance(c, int):
                    act.wait_ge(act_ready, base(phase) + c)
                act.activation(gate_s[:, :], flat(pair[0]), ACT.Silu).then_inc(silu_done, 1)

            def ffn_side(phase):
                u0 = FIRST[phase]
                for i in range(2 * KG):
                    split(u0 + i + LEAD)
                    if i == KG - 1:
                        silu(phase, 0, u0 + i)
                with act.Fori(1, CH) as c:
                    u = u0 + 2 * KG + (c - 1) * 12
                    for j in range(12):
                        i = 2 * KG + j + LEAD
                        split_hi(u + j + LEAD, i % SPLIT, i % RAW, (c - 1) * (12 // RAW) + (u0 + i) // RAW + 1)
                        if j == 1:
                            split_activation(phase, c - 1)
                        if j == KG - 1:
                            silu(phase, c, u + j)
                split_activation(phase, CH - 1)
                for g in range(NG):
                    split(u0 + FFN_UNITS - NG + g + LEAD)
                    if phase == "ffn1":
                        square_final_x(phase, 2 * NG * (CH - 1) + 2 * g)

            def z_done(name):
                act.wait_ge(unit_done, FIRST["mix"] + 4 * CHUNK_OF[name] + 4)

            def wait_work(name):
                act.wait_ge(work_ready, up_to(WORK, name))

            def root(name, n=NTOK * HEADS):
                act.wait_ge(head_mean, up_to(STATS, name))
                act.activation(hst[:, 2, 0:n], hst[:, 1, 0:n], ACT.Sqrt).then_inc(head_root, 1)

            def exps(k, a, s, width):
                act.wait_ge(score_max, k)
                for h in range(HEADS):
                    act.activation(s[:, h, :], s[:, h, :], ACT.Exp, bias=sst[:, 2, h:h + 1],
                                   accum_out=sst[:, 4, h:h + 1])
                act.activation(sst[:, 5, :], sst[:, 3, :], ACT.Exp).then_inc(exp_done, 1)

            def copy_work(name, to, n):
                wait_work(name)
                act.activation(to, work[:, 0:n], ACT.Copy).then_inc(work_free, 1)

            def side(what):
                kind, _, name = what.partition(" ")
                if what == "ka":
                    z_done("kv")
                    z = pair[CHUNK_OF["kv"] % 2]
                    act.activation(va[:, :, :], z[:, :, 2 * HD:4 * HD], ACT.Copy).then_inc(v_copied, 1)
                    act.activation(square[:, 0:4 * HD].rearrange("p (t n) -> p t n", t=NTOK),
                                   z[:, :, 0:2 * HD], ACT.Square).then_inc(head_sq, 1)
                    root("ka", 4)
                elif what in ("qa0", "qa1"):
                    z_done(what)
                    act.activation(square[:, :], flat(pair[CHUNK_OF[what] % 2]), ACT.Square).then_inc(head_sq, 1)
                    root(what)
                elif kind == "T":
                    to = {"ka": kaT, "kr0": krT, "kr1": krT}.get(name, qT)
                    copy_work(what, to[:, :, :].rearrange("p h n -> p (h n)"), 2 * SEQ if name == "ka" else HEADS * SEQ)
                elif kind == "S1":
                    exps(2 * int(name[1]) + 1, int(name[1]), s1, SEQ)
                elif kind == "S0":
                    exps(2 * int(name[1]) + 2, int(name[1]), s0, P)
                elif kind == "PT1":
                    copy_work(what, t1[:, :, :].rearrange("p h n -> p (h n)"), 2 * HEADS * P)
                elif kind == "PT0":
                    copy_work(what, t0[:, :, :].rearrange("p h n -> p (h n)"), HEADS * P)
                elif kind in ("PV", "TY"):
                    wait_work(what)
                    act.activation(aT_hi[:, int(name[1]), :], work, ACT.Copy).then_inc(mT_hi_done, 1)
                elif what in ("vr0", "vr1"):
                    z_done(what)
                    if what == "vr1":
                        wait_work("Y r0")
                    act.activation(vr[:, :, :], pair[CHUNK_OF[what] % 2], ACT.Copy).then_inc(z_free_s, 1)
                elif kind == "Y":
                    wait_work(what)
                    act.activation(square[:, :], work, ACT.Square).then_inc(head_sq, 1)
                    root("y " + name)
                elif what in ("gr0", "gr1"):
                    z_done(what)
                    if what == "gr0":
                        act.wait_ge(act_ready, CH)
                    else:
                        act.wait_ge(rows_ready, up_to(ROWS, "y r0"))
                    act.activation(gate_s[:, :], flat(pair[CHUNK_OF[what] % 2]), ACT.Silu).then_inc(z_free_s, 1)

            def mixer_side():
                for t in range(MIX_UNITS):
                    split(FIRST["mix"] + t + LEAD)
                    for what in AFTER.get(t, ()):
                        side(what)
                    if t // 4 == CHUNK_OF["r1"]:
                        square_final_x("mix", 2 * NG * (len(OUTS) - 1) + 2 * (t % 4))

            for g in range(NG):
                act.wait_ge(x_landed[g], 16)
                square_x(0, g)
            norm(0, range(LEAD))
            ffn_side("ffn1")
            norm(1, ())
            mixer_side()
            norm(2, ())
            ffn_side("ffn2")

        @block.vector
        def _(dve):
            links = [0]

            def mark(ins):
                links[0] += 1
                ins.then_inc(chain, 1)

            def settle():
                dve.wait_ge(chain, links[0])

            def split_lo(u, slot, raw_slot):
                dve.wait_ge(hi_done, u + 1)
                dve.tensor_tensor(w_lo[:, slot, :, :], raw[:, raw_slot, :, :], w_hi[:, slot, :, :].bitcast(F32),
                                  ALU.subtract).then_inc(lo_done, 1)

            def split(u):
                if u < UNITS:
                    split_lo(u, u % SPLIT, u % RAW)

            def norm(n, early):
                dve.wait_ge(squared, NTOK * NG * (n + 1))
                mark(dve.tensor_reduce(nst[:, 0:2], ssq[:, :, :], AX_X, ALU.add))
                settle()
                dve.tensor_scalar(nst[:, 2:4], nst[:, 0:2], 1.0 / D_MODEL, EPS, ALU.mult, ALU.add).then_inc(mean_ready, 1)
                dve.wait_ge(root_ready, n + 1)
                mark(dve.reciprocal(nst[:, 6:8], nst[:, 4:6]))
                settle()
                dve.wait_ge(table_landed, [16, 32, 64][n])

                def low(g):
                    dve.wait_ge(hT_hi_done, n * KG + g + 1)
                    dve.tensor_tensor(hT_lo[:, g, :], flat(sums[:, 2 * (g % 2):2 * (g % 2) + 2, :]),
                                      hT_hi[:, g, :].bitcast(F32), ALU.subtract).then_inc(hT_lo_done, 1)

                for g in range(KG):
                    if g >= 2:
                        dve.wait_ge(hT_raw, n * KG + g - 1)
                    for t in range(NTOK):
                        dve.scalar_tensor_tensor(out=rows[:, g % 2, t * UW:(t + 1) * UW],
                                                 in0=xs[:, t, g * UW:(g + 1) * UW], scalar=nst[:, 6 + t:7 + t],
                                                 in1=table[:, g * UW:(g + 1) * UW], op0=ALU.mult,
                                                 op1=ALU.mult).then_inc(normed, 1)
                    if g < len(early):
                        split(early[g])
                    if g >= 1:
                        low(g - 1)
                low(KG - 1)

            def add_sums(phase, u, g, s, to, scale):
                for t in range(NTOK):
                    if t == 0:
                        dve.wait_ge(half_done, (sums_before(phase) + s) // 2 + 1)
                    else:
                        dve.wait_ge(unit_done, u + 1)
                    part = xs[:, t, g * UW:(g + 1) * UW]
                    dve.scalar_tensor_tensor(out=part, in0=to[t], scalar=scale, in1=part, op0=ALU.mult,
                                             op1=ALU.add).then_inc(sum_room, 1)

            def split_activation(phase, c, which=0):
                dve.wait_ge(aT_hi_done, base(phase) + c + 1)
                dve.tensor_tensor(aT_lo[:, which, :], flat(pair[1]), aT_hi[:, which, :].bitcast(F32),
                                  ALU.subtract).then_inc(aT_lo_done, 1)

            def multiply_up(phase, c, u):
                dve.wait_ge(unit_done, u + 1)
                dve.wait_ge(silu_done, base(phase) + c + 1)
                dve.tensor_tensor(act_s[:, :], flat(pair[1]), gate_s[:, :], ALU.mult).then_inc(act_ready, 1)

            def ffn_side(phase):
                u0 = FIRST[phase]
                for i in range(2 * KG):
                    split(u0 + i + LEAD)
                    if i == 2 * KG - 1:
                        multiply_up(phase, 0, u0 + i)
                with dve.Fori(1, CH) as c:
                    u = u0 + 2 * KG + (c - 1) * 12
                    for j in range(12):
                        i = 2 * KG + j + LEAD
                        split_lo(u + j + LEAD, i % SPLIT, i % RAW)
                        if j == 1:
                            split_activation(phase, c - 1)
                        if j == 2 * KG - 1:
                            multiply_up(phase, c, u + j)
                        if j >= 2 * KG:
                            g = j - 2 * KG
                            dve.wait_ge(half_done, sums_before(phase) // 2 + NG * (c - 1) + g + 1)
                            for t in range(NTOK):
                                if t == 1:
                                    dve.wait_ge(unit_done, u + j + 1)
                                part = xs[:, t, g * UW:(g + 1) * UW]
                                dve.scalar_tensor_tensor(out=part, in0=sums[:, (2 * g + t) % 4, :], scalar=0.5,
                                                         in1=part, op0=ALU.mult, op1=ALU.add).then_inc(sum_room, 1)
                split_activation(phase, CH - 1)
                for g in range(NG):
                    u = u0 + FFN_UNITS - NG + g
                    split(u + LEAD)
                    add_sums(phase, u, g, 2 * NG * (CH - 1) + 2 * g,
                             [sums[:, (2 * g) % 4, :], sums[:, (2 * g + 1) % 4, :]], 0.5)

            def wait_work(name):
                dve.wait_ge(work_ready, up_to(WORK, name))

            def own_rows(name):
                if ROWS.index(name):
                    dve.wait_ge(rows_ready, ROWS.index(name))

            def head_stats(name, n):
                dve.wait_ge(head_sq, up_to(STATS, name))
                mark(dve.tensor_reduce(hst[:, 0, 0:n], square[:, 0:n * HD].rearrange("p (h d) -> p h d", d=HD),
                                       AX_X, ALU.add))
                settle()
                dve.tensor_scalar(hst[:, 1, 0:n], hst[:, 0, 0:n], 1.0 / HD, EPS, ALU.mult,
                                  ALU.add).then_inc(head_mean, 1)
                dve.wait_ge(head_root, up_to(STATS, name))
                mark(dve.reciprocal(hst[:, 3, 0:n], hst[:, 2, 0:n]))
                settle()

            def each(a, n, d):
                return a.unsqueeze(2).to_broadcast([P, n, d])

            def norm_heads(name, heads, gain, buf, last_use):
                n = NTOK * heads
                z = pair[CHUNK_OF["kv" if name == "ka" else name] % 2][:, :, 0:heads * HD]
                out_rows = rows[:, buf, 0:n * HD]
                if last_use:
                    wait_work(last_use)
                own_rows(name)
                head_stats(name, n)
                r4 = out_rows.rearrange("p (t h d) -> p t h d", t=NTOK, h=heads)
                dve.tensor_tensor(r4, z.rearrange("p t (h d) -> p t h d", d=HD),
                                  hst[:, 3, 0:n].rearrange("p (t h) -> p t h", t=NTOK).unsqueeze(3)
                                  .to_broadcast([P, NTOK, heads, HD]), ALU.mult).then_inc(z_free_v, 1)
                dve.wait_ge(z_free_v, up_to(Z_VECTOR, "kv" if name == "ka" else name))
                rf = out_rows.rearrange("p (h d) -> p h d", d=HD)
                mark(dve.tensor_tensor(rf, rf, gain[:, :].unsqueeze(1).to_broadcast([P, n, HD]), ALU.mult))
                settle()
                half = ROPE // 2
                turned = act_s[:, 0:n * ROPE].rearrange("p (t h d) -> p t h d", t=NTOK, h=heads)
                over = lambda a, w: a.unsqueeze(2).to_broadcast([P, NTOK, heads, w])
                mark(dve.tensor_tensor(turned[:, :, :, 0:half], r4[:, :, :, half:ROPE],
                                       over(sin_a[:, :, 0:half], half), ALU.mult))
                mark(dve.tensor_tensor(turned[:, :, :, half:ROPE], r4[:, :, :, 0:half],
                                       over(sin_a[:, :, half:ROPE], half), ALU.mult))
                settle()
                mark(dve.tensor_tensor(r4[:, :, :, 0:ROPE], r4[:, :, :, 0:ROPE], over(cos_a, ROPE), ALU.mult))
                settle()
                dve.tensor_tensor(r4[:, :, :, 0:ROPE], r4[:, :, :, 0:ROPE], turned, ALU.add).then_inc(rows_ready, 1)

            def rotate_heads(name, buf, last_use):
                z = pair[CHUNK_OF[name] % 2].rearrange("p t (h d) -> p t h d", d=HD)
                dve.wait_ge(unit_done, FIRST["mix"] + 4 * CHUNK_OF[name] + 4)
                own_rows(name)
                if last_use:
                    wait_work(last_use)
                half = HD // 2
                r4 = rows[:, buf, :].rearrange("p (t h d) -> p t h d", t=NTOK, h=HEADS)
                turned = act_s[:, :].rearrange("p (t h d) -> p t h d", t=NTOK, h=HEADS)
                over = lambda a, w: a.unsqueeze(2).to_broadcast([P, NTOK, HEADS, w])
                mark(dve.tensor_tensor(r4, z, over(cos_r, HD), ALU.mult))
                mark(dve.tensor_tensor(turned[:, :, :, 0:half], z[:, :, :, half:HD],
                                       over(sin_r[:, :, 0:half], half), ALU.mult))
                dve.tensor_tensor(turned[:, :, :, half:HD], z[:, :, :, 0:half],
                                  over(sin_r[:, :, half:HD], half), ALU.mult).then_inc(z_free_v, 1)
                settle()
                dve.wait_ge(z_free_v, up_to(Z_VECTOR, name))
                dve.tensor_tensor(r4, r4, turned, ALU.add).then_inc(rows_ready, 1)

            def softmax(what, k, a, s, width, masked):
                wait_work(what)
                own_rows(what.replace("S", "P"))
                dve.scalar_tensor_tensor(out=s[:, :, :], in0=work[:, 0:HEADS * width].rearrange("p (h n) -> p h n", n=width),
                                         scalar=float(HD) ** -0.5,
                                         in1=masked.unsqueeze(1).to_broadcast([P, HEADS, width]),
                                         op0=ALU.mult, op1=ALU.add).then_inc(work_free, 1)
                dve.wait_ge(work_free, up_to(WORK, what))
                mark(dve.tensor_reduce(sst[:, 0, :], s[:, :, :], AX_X, ALU.max))
                settle()
                sinks4 = sink[:, a * HEADS:(a + 1) * HEADS]
                mark(dve.tensor_tensor(sst[:, 1, :], sst[:, 0, :], sinks4, ALU.max))
                settle()
                mark(dve.tensor_scalar(sst[:, 2, :], sst[:, 1, :], -1.0, None, ALU.mult))
                dve.tensor_tensor(sst[:, 3, :], sinks4, sst[:, 1, :], ALU.subtract).then_inc(score_max, 1)
                dve.wait_ge(exp_done, k)
                mark(dve.tensor_tensor(sst[:, 6, :], sst[:, 4, :], sst[:, 5, :], ALU.add))
                settle()
                mark(dve.reciprocal(sst[:, 7, :], sst[:, 6, :]))
                settle()
                dve.tensor_tensor(s[:, :, :], s[:, :, :], each(sst[:, 7, :], HEADS, width),
                                  ALU.mult).then_inc(rows_ready, 1)

            def decayed(what, r, to, width):
                wait_work(what)
                dve.wait_ge(table_landed, 48)
                dve.tensor_tensor(to[:, :, :].rearrange("p a n -> p (a n)").rearrange("p (h n) -> p h n", h=HEADS),
                                  work[:, 0:HEADS * width].rearrange("p (h n) -> p h n", n=width),
                                  decays[:, r * HEADS:(r + 1) * HEADS, 0:width], ALU.mult).then_inc(work_free, 1)

            def side(what):
                kind, _, name = what.partition(" ")
                if what == "ka":
                    dve.wait_ge(const_landed, 64)
                    norm_heads("ka", 2, kgain, 0, None)
                elif what == "qa0":
                    norm_heads("qa0", HEADS, qgain, 0, "T ka")
                elif what == "qa1":
                    norm_heads("qa1", HEADS, qgain, 0, "T qa0")
                elif what == "qr0":
                    rotate_heads(what, 1, None)
                elif what == "kr0":
                    rotate_heads(what, 0, "T qa1")
                elif what == "qr1":
                    rotate_heads(what, 0, "T kr0")
                elif what == "kr1":
                    rotate_heads(what, 1, "TY r0")
                elif kind == "S1":
                    a = int(name[1])
                    softmax(what, 2 * a + 1, a, s1, SEQ, mask)
                elif kind == "S0":
                    a = int(name[1])
                    softmax(what, 2 * a + 2, a, s0, P, mask[:, P:SEQ])
                elif kind in ("PV", "TY"):
                    dve.wait_ge(mT_hi_done, up_to(OUTS, name))
                    dve.tensor_tensor(aT_lo[:, int(name[1]), :], work, aT_hi[:, int(name[1]), :].bitcast(F32),
                                      ALU.subtract).then_inc(work_free, 1)
                elif kind == "R1":
                    decayed(what, int(name[1]), t1, SEQ)
                elif kind == "R0":
                    decayed(what, int(name[1]), t0, P)
                elif kind == "Y":
                    buf, last_use = {"r0": (1, "T qr0"), "r1": (0, "T qr1")}[name]
                    wait_work(last_use)
                    head_stats("y " + name, NTOK * HEADS)
                    dve.tensor_tensor(rows[:, buf, :].rearrange("p (h d) -> p h d", d=HD),
                                      work.rearrange("p (h d) -> p h d", d=HD),
                                      each(hst[:, 3, :], NTOK * HEADS, HD), ALU.mult).then_inc(work_free, 1)
                elif what in ("gr0", "gr1"):
                    buf = {"gr0": 1, "gr1": 0}[what]
                    dve.wait_ge(z_free_s, up_to(Z_SCALAR, what))
                    dve.wait_ge(work_free, up_to(WORK, "Y " + what[1:]))
                    dve.tensor_tensor(rows[:, buf, :], rows[:, buf, :], gate_s[:, :], ALU.mult).then_inc(rows_ready, 1)

            def mixer_side():
                for t in range(MIX_UNITS):
                    split(FIRST["mix"] + t + LEAD)
                    s, g = divmod(t, 4)
                    kind, name, _ = MIX[s]
                    if kind == "out":
                        two = pair[s % 2] if g % 2 == 0 else sums[:, 0:2, :]
                        add_sums("mix", FIRST["mix"] + t, g, 2 * NG * OUTS.index(name) + 2 * g,
                                 [two[:, 0, :], two[:, 1, :]], 1.0)
                    for what in AFTER.get(t, ()):
                        side(what)

            for i in range(4):
                dve.memset(spare[:, i:i + 1], 0.0).then_inc(sum_room, 1)
            norm(0, range(LEAD))
            ffn_side("ffn1")
            norm(1, ())
            mixer_side()
            norm(2, ())
            ffn_side("ffn2")


def tables():
    import numpy as np
    f32 = np.float32

    def rotary(dim, theta):
        inv = f32(theta) ** (-np.arange(0, dim, 2, dtype=f32) / f32(dim))
        ang = np.arange(SEQ, dtype=f32)[:, None] * inv[None, :]
        cos, sin = np.cos(ang), np.sin(ang)
        both = np.concatenate([cos, cos], 1), np.concatenate([-sin, sin], 1)
        return [a.reshape(NTOK, P, dim).transpose(1, 0, 2).reshape(P, NTOK * dim) for a in both]

    i, j = np.arange(P)[:, None], np.arange(SEQ)[None, :]
    mask = np.where((j > i) & (j <= P + i), 0.0, NEG)
    const = np.concatenate([np.eye(P), *rotary(HD, 10000.0), *rotary(ROPE, 500000.0), mask], 1).astype(f32)
    gamma = 1.0 - 2.0 ** (-5.0 - np.arange(2 * HEADS))
    ago = j - i
    decay = np.where(ago >= 0, gamma[:, None, None] ** np.maximum(ago, 0), 0.0) * HD ** -0.5
    return const, np.ascontiguousarray(decay.transpose(1, 0, 2).reshape(P, -1).astype(f32))


_INS = ["x", "ffn1_norm", "mix_norm", "ffn2_norm", "ffn1_w_gate", "ffn1_w_up", "ffn1_w_down",
        "ffn2_w_gate", "ffn2_w_up", "ffn2_w_down", "w_in", "w_out", "q_norm", "k_norm", "attn_sinks"]


def kernel(**inputs):
    import numpy as np
    import concourse.bacc as bacc
    from concourse.bass_utils import run_bass_kernel_spmd

    const, decay = tables()
    arrays = {name: np.ascontiguousarray(inputs[name]) for name in _INS}
    arrays["consts"], arrays["decays"] = const, decay
    nc = bacc.Bacc("TRN2", target_bir_lowering=False, num_devices=1)
    d = {name: nc.dram_tensor(f"in_{name}", a.shape, mybir.dt.from_np(a.dtype), kind="ExternalInput").ap()
         for name, a in arrays.items()}
    out = nc.dram_tensor("out_x", (1, SEQ, D_MODEL), F32, kind="ExternalOutput").ap()
    build(nc, d["x"], [d["ffn1_norm"], d["mix_norm"], d["ffn2_norm"]],
          {f: (d[f + "_w_gate"], d[f + "_w_up"], d[f + "_w_down"]) for f in ("ffn1", "ffn2")},
          d["w_in"], d["w_out"], d["q_norm"], d["k_norm"], d["attn_sinks"], d["consts"], d["decays"], out)
    r = run_bass_kernel_spmd(nc, [{f"in_{name}": a for name, a in arrays.items()}], core_ids=[0])
    return r.results[0]["out_x"]
```

```python
from contextlib import ExitStack

import concourse.bass as bass
from concourse import mybir

F32 = mybir.dt.float32
F32R = mybir.dt.float32r
ACT = mybir.ActivationFunctionType
ALU = mybir.AluOpType
AX_X = mybir.AxisListType.X

P = 128
EPS = 1e-6
NEG = -1e30

D_MODEL = 2048
SEQ = 256
D_FF = 5632
HD = 128
ROPE = 32
NTOK = SEQ // P
UW = 512
KT = UW // P
KG = D_MODEL // UW
NG = D_MODEL // UW
CH = D_FF // UW
HEADS = UW // HD
RAW = 4
SPLIT = 3
WARM = 16
LEAD = SPLIT - 1
EARLY = 5

MIX = [("in", "kv", 5120), ("in", "qa0", 4096), ("in", "qa1", 4608),
       ("in", "qr0", 0), ("in", "kr0", 1024), ("in", "vr0", 2048), ("out", "a0", 1024),
       ("in", "gr0", 3072), ("in", "qr1", 512), ("in", "kr1", 1536), ("out", "a1", 1536),
       ("in", "vr1", 2560), ("in", "gr1", 3584), ("out", "r0", 0), ("out", "r1", 512)]
CHUNK_OF = {name: s for s, (_, name, _) in enumerate(MIX)}
OUTS = [name for kind, name, _ in MIX if kind == "out"]

FFN_UNITS = CH * (2 * KG + NG)
MIX_UNITS = 4 * len(MIX)
FIRST = {"ffn1": 0, "mix": FFN_UNITS, "ffn2": FFN_UNITS + MIX_UNITS}
UNITS = 2 * FFN_UNITS + MIX_UNITS

WORK = ["T ka", "T qa0", "S1 a0", "S0 a0", "PT1 a0", "PT0 a0", "PV a0", "T qa1", "S1 a1", "S0 a1",
        "T qr0", "PT1 a1", "PT0 a1", "PV a1", "T kr0", "R1 r0", "R0 r0", "Y r0", "TY r0",
        "T qr1", "T kr1", "R1 r1", "R0 r1", "Y r1", "TY r1"]
ROWS = ["ka", "qa0", "P1 a0", "P0 a0", "qa1", "qr0", "P1 a1", "P0 a1", "kr0", "y r0", "qr1", "kr1", "y r1"]
STATS = ["ka", "qa0", "qa1", "y r0", "y r1"]
Z_VECTOR = ["kv", "qa0", "qa1", "qr0", "kr0", "qr1", "kr1"]
Z_SCALAR = ["vr0", "gr0", "vr1", "gr1"]
AFTER = {3: ["ka"], 5: ["T ka"], 7: ["qa0"], 9: ["T qa0"], 10: ["S1 a0"], 11: ["S0 a0"],
         13: ["PT1 a0", "qa1"], 14: ["PT0 a0"], 15: ["PV a0", "qr0"], 16: ["T qa1"], 17: ["S1 a1"],
         18: ["S0 a1"], 19: ["T qr0", "kr0"], 20: ["PT1 a1"], 21: ["PT0 a1"], 22: ["PV a1"],
         23: ["T kr0", "vr0"], 24: ["R1 r0"], 25: ["R0 r0"], 26: ["Y r0"], 31: ["gr0"], 33: ["TY r0"],
         35: ["qr1"], 37: ["T qr1"], 39: ["kr1"], 41: ["T kr1"], 42: ["R1 r1"], 43: ["R0 r1"],
         47: ["vr1"], 48: ["Y r1"], 51: ["gr1"], 53: ["TY r1"]}

C_ID, C_COSA, C_SINA, C_MASK, C_TURN = 0, 128, 192, 256, 512
C_ALL = 1024


def build(nc, x, xT, gain_cols, gains, ffn, w_in, w_out, q_norm, k_norm, sinks, consts, decay, out):
    with ExitStack() as ctx:
        def sb(name, shape, dt=F32):
            return ctx.enter_context(nc.sbuf_tensor(name, shape, dt))

        def sem(name):
            return ctx.enter_context(nc.semaphore(name))

        raw = sb("raw", [P, RAW, KT, UW])
        w_hi = sb("w_hi", [P, SPLIT, KT, UW], F32R)
        w_lo = sb("w_lo", [P, SPLIT, KT, UW], F32R)
        xs = sb("xs", [P, NTOK, D_MODEL])
        hT_hi = sb("hT_hi", [P, KG, KT * SEQ], F32R)
        hT_lo = sb("hT_lo", [P, KG, KT * SEQ], F32R)
        aT_hi = sb("aT_hi", [P, 2, KT * SEQ], F32R)
        aT_lo = sb("aT_lo", [P, 2, KT * SEQ], F32R)
        gate_s = sb("gate_s", [P, NTOK * UW])
        act_s = sb("act_s", [P, NTOK * UW])
        table = sb("table", [P, D_MODEL])
        rows = sb("rows", [P, 2, NTOK * UW])
        square = sb("square", [P, NTOK * UW])
        kaT = sb("kaT", [P, 2, SEQ])
        qT = sb("qT", [P, HEADS, SEQ])
        krT = sb("krT", [P, HEADS, SEQ])
        s1 = sb("s1", [P, HEADS, SEQ])
        s0 = sb("s0", [P, HEADS, P])
        t1 = sb("t1", [P, 2 * HEADS, P])
        t0 = sb("t0", [P, HEADS, P])
        va = sb("va", [P, NTOK, 2 * HD])
        vr = sb("vr", [P, NTOK, UW])
        const = sb("const", [P, C_ALL])
        gcol = sb("gcol", [P, D_MODEL // P])
        qgain = sb("qgain", [P, HD])
        kgain = sb("kgain", [P, HD])
        sink = sb("sink", [P, 2 * HEADS])
        ssq = sb("ssq", [P, NTOK, NG])
        nst = sb("nst", [P, 4 * NTOK])
        hst = sb("hst", [P, 4, 2 * HEADS])
        sst = sb("sst", [P, 8, HEADS])

        spare = sb("spare", [P, 4])

        banks = ctx.enter_context(nc.psum_tensor("banks", [P, 8, UW], F32))

        x_landed = [sem(f"x_landed{n}") for n in range(NG)]
        xT_landed = [sem(f"xT_landed{g}") for g in range(KG)]
        gcol_landed = sem("gcol_landed")
        zeroed = sem("zeroed")
        gain_landed = [sem(f"gain_landed{g}") for g in range(KG)]
        decay_landed = sem("decay_landed")
        ident_landed = sem("ident_landed")
        const_landed = sem("const_landed")
        raw_landed = [sem(f"raw_landed{s}") for s in range(RAW)]
        hi_done = sem("hi_done")
        lo_done = sem("lo_done")
        unit_done = sem("unit_done")
        squared = sem("squared")
        mean_ready = sem("mean_ready")
        root_ready = sem("root_ready")
        gained = sem("gained")
        rms_ready = sem("rms_ready")
        hT_raw = sem("hT_raw")
        hT_hi_done = sem("hT_hi_done")
        hT_lo_done = sem("hT_lo_done")
        silu_done = sem("silu_done")
        act_ready = sem("act_ready")
        aT_raw = sem("aT_raw")
        aT_hi_done = sem("aT_hi_done")
        aT_lo_done = sem("aT_lo_done")
        mT_hi_done = sem("mT_hi_done")
        half_done = sem("half_done")
        sum_room = sem("sum_room")
        z_free_v = sem("z_free_v")
        z_free_s = sem("z_free_s")
        work_ready = sem("work_ready")
        work_free = sem("work_free")
        rows_ready = sem("rows_ready")
        head_sq = sem("head_sq")
        head_mean = sem("head_mean")
        head_root = sem("head_root")
        score_max = sem("score_max")
        exp_done = sem("exp_done")
        v_copied = sem("v_copied")
        chain = sem("chain")
        stored = sem("stored")

        ident = const[:, C_ID:C_ID + P]
        turn = const[:, C_TURN:C_TURN + NTOK * 2 * HD].rearrange("p (t c d) -> p t c d", t=NTOK, c=2)
        cos_r, sin_r = turn[:, :, 0, :], turn[:, :, 1, :]
        rms = nst[:, 6:8]
        cos_a = const[:, C_COSA:C_COSA + NTOK * ROPE].rearrange("p (t d) -> p t d", t=NTOK)
        sin_a = const[:, C_SINA:C_SINA + NTOK * ROPE].rearrange("p (t d) -> p t d", t=NTOK)
        mask = const[:, C_MASK:C_MASK + SEQ]
        decays = table[:, :].rearrange("p (h n) -> p h n", n=SEQ)

        pair = [banks[:, 0:2, :], banks[:, 2:4, :]]
        sums = banks[:, 4:8, :]
        work = banks[:, 6:8, :].rearrange("p b n -> p (b n)")
        flat = lambda a: a.rearrange("p b n -> p (b n)")

        x_d = x.rearrange("o (t p) n -> p (o t) n", p=P)
        out_d = out.rearrange("o (t p) n -> p (o t) n", p=P)

        def base(phase):
            return 0 if phase == "ffn1" else CH

        def sums_before(phase):
            return {"ffn1": 0, "mix": 2 * NG * CH, "ffn2": 2 * NG * (CH + len(OUTS))}[phase]

        def up_to(names, name):
            return names.index(name) + 1

        block = ctx.enter_context(nc.Block())

        @block.sync
        def _(sp):
            def load_x(g):
                sp.dma_start(xs[:, :, g * UW:(g + 1) * UW], x_d[:, :, g * UW:(g + 1) * UW]).then_inc(x_landed[g], 16)

            def load_gain(n, g):
                cols = slice(g * UW, (g + 1) * UW)
                sp.dma_start(table[:, cols], gains[n - 1][0, cols].partition_broadcast(P)).then_inc(gain_landed[g], 16)

            def load(u, slot, src, at=None):
                if at is not None or u >= RAW:
                    sp.wait_ge(lo_done, (u if at is None else at) - RAW + 1)
                sp.dma_start(raw[:, slot, :, :].rearrange("p k n -> p (k n)"), src).then_inc(raw_landed[slot], 16)

            def load_ffn(phase):
                gate, up, down = ffn[phase]
                u0 = FIRST[phase]
                for g in range(KG):
                    load(u0 + g, g % RAW, gate[0, g])
                    if phase == "ffn1":
                        if g == 0:
                            sp.dma_start(gcol[:, :], gain_cols).then_inc(gcol_landed, 16)
                        if g >= 2:
                            sp.wait_ge(hT_lo_done, g - 1)
                        sp.dma_start(rows[:, g % 2, :], xT[g]).then_inc(xT_landed[g], 16)
                for g in range(KG):
                    if phase == "ffn1" and KG + g == EARLY:
                        for column_group in range(NG):
                            load_x(column_group)
                        sp.dma_start(const[:, 0:P], consts[:, 0:P]).then_inc(ident_landed, 16)
                    load(u0 + KG + g, g % RAW, up[0, g])
                if phase == "ffn1":
                    sp.dma_start(const[:, P:C_ALL], consts[:, P:C_ALL]).then_inc(const_landed, 16)
                    sp.dma_start(qgain[:, :], q_norm[0].partition_broadcast(P)).then_inc(const_landed, 16)
                    sp.dma_start(kgain[:, :], k_norm[0].partition_broadcast(P)).then_inc(const_landed, 16)
                    sp.dma_start(sink[:, :], sinks[0].partition_broadcast(P)).then_inc(const_landed, 16)
                    for g in range(KG):
                        load_gain(1, g)
                with sp.Fori(1, CH) as c:
                    first = u0 + 2 * KG + (c - 1) * 12
                    for g in range(KG):
                        load(None, g % RAW, gate[c, g], first + g)
                    for g in range(KG):
                        load(None, g % RAW, up[c, g], first + KG + g)
                    for g in range(NG):
                        load(None, g % RAW, down[c - 1, g], first + 2 * KG + g)
                for g in range(NG):
                    u = u0 + FFN_UNITS - NG + g
                    load(u, u % RAW, down[CH - 1, g])

            load_ffn("ffn1")
            for s, (kind, name, at) in enumerate(MIX):
                for g in range(4):
                    u = FIRST["mix"] + 4 * s + g
                    load(u, u % RAW, (w_in if kind == "in" else w_out)[at // UW, g])
                if name == "qa0":
                    sp.wait_ge(gained, KG)
                    sp.dma_start(table[:, :], decay).then_inc(decay_landed, 16)
                if name == "r0":
                    sp.wait_ge(work_free, up_to(WORK, "R0 r1"))
                    for g in range(KG):
                        load_gain(2, g)
            load_ffn("ffn2")
            for g in range(NG):
                for t in range(NTOK):
                    sp.wait_ge(sum_room, 4 + sums_before("ffn2") + 2 * NG * (CH - 1) + 2 * g + t + 1)
                    cols = slice(g * UW, (g + 1) * UW)
                    sp.dma_start(out_d[:, t, cols], xs[:, t, cols]).then_inc(stored, 16)
            sp.wait_ge(stored, 16 * NG * NTOK)

        @block.gpsimd
        def _(pool):
            pool.memset(krT[:, 0, :], 0.0).then_inc(zeroed, 1)

        @block.tensor
        def _(pe):
            def product(slot, left, t, to, start, stop):
                left_hi, left_lo = left
                for k in range(KT):
                    cols = slice((k * NTOK + t) * P, (k * NTOK + t + 1) * P)
                    for n, (a, b) in enumerate(((left_hi, w_hi), (left_hi, w_lo), (left_lo, w_hi))):
                        last = pe.matmul(to, a[:, cols], b[:, slot, k, :],
                                         start=start and k == 0 and n == 0,
                                         stop=stop and k == KT - 1 and n == 2)
                return last

            def columns(u, slot, g, to, between=None):
                pe.wait_ge(lo_done, u + 1)
                left = hT_hi[:, g, :], hT_lo[:, g, :]
                for t in range(NTOK):
                    if t and between:
                        norm_transposes(*between)
                    last = product(slot, left, t, to[:, t, :], g == 0, g == KG - 1)
                last.then_inc(unit_done, 1)

            def transpose(to, of, n):
                for i in range(n):
                    last = pe.transpose(to(i), of(i), ident)
                return last

            def rows_sum(u, slot, which, first_sum, to):
                pe.wait_ge(lo_done, u + 1)
                left = aT_hi[:, which, :], aT_lo[:, which, :]
                pe.wait_ge(sum_room, first_sum + 1)
                product(slot, left, 0, to[0], True, True).then_inc(half_done, 1)
                pe.wait_ge(sum_room, first_sum + 2)
                product(slot, left, 1, to[1], True, True).then_inc(unit_done, 1)

            def norm_transposes(n, g):
                pe.wait_ge(gained, (n - 1) * KG + g + 1)
                if g:
                    pe.wait_ge(hT_lo_done, n * KG + g)
                at = lambda i: flat(pair[1])[:, i * P:(i + 1) * P]
                of = lambda i: rows[:, g % 2, ((i % 2) * KT + i // 2) * P:((i % 2) * KT + i // 2 + 1) * P]
                transpose(at, of, KT * NTOK).then_inc(hT_raw, 1)

            def first_chunk(n, u0):
                if n == 0:
                    pe.wait_ge(zeroed, 1)
                    for _ in range(WARM):
                        pe.matmul(pair[0][:, 0, 0:SEQ], krT[:, 0, 0:P], krT[:, 0, :], start=True, stop=True)
                for g in range(KG):
                    pe.wait_ge(hT_lo_done, n * KG + g + 1)
                    between = (n, KG - 1) if n and g == 1 else None
                    columns(u0 + g, (u0 + g) % SPLIT, g, pair[0], between)

            def activation_transposes(phase, c, which=0):
                pe.wait_ge(act_ready, base(phase) + c + 1)
                at = lambda i: flat(pair[1])[:, i * P:(i + 1) * P]
                of = lambda i: act_s[:, ((i % 2) * KT + i // 2) * P:((i % 2) * KT + i // 2 + 1) * P]
                transpose(at, of, KT * NTOK).then_inc(aT_raw, 1)

            def multiply_ffn(phase, n):
                u0 = FIRST[phase]
                first_chunk(n, u0)
                for g in range(KG):
                    columns(u0 + KG + g, (u0 + KG + g) % SPLIT, g, pair[1])

                def chunk(c, last=False):
                    u = u0 + 2 * KG + (c - 1) * 12
                    done = base(phase) + c
                    pe.wait_ge(silu_done, done)
                    for g in range(KG):
                        columns(u + g, (2 * KG + g) % SPLIT, g, pair[0])
                        if g == 1:
                            activation_transposes(phase, c - 1)
                    pe.wait_ge(aT_lo_done, done)
                    for g in range(KG):
                        columns(u + KG + g, (3 * KG + g) % SPLIT, g, pair[1])
                    for g in range(NG):
                        s = sums_before(phase) + 2 * NG * (c - 1) + 2 * g
                        rows_sum(u + 2 * KG + g, (4 * KG + g) % SPLIT, 0, s,
                                 [sums[:, (2 * g) % 4, :], sums[:, (2 * g + 1) % 4, :]])
                        if last and g == 1:
                            activation_transposes(phase, c)

                if phase == "ffn1":
                    pe.wait_ge(ident_landed, 16)
                with pe.Fori(1, CH - 1) as c:
                    chunk(c)
                chunk(CH - 1, last=True)
                pe.wait_ge(aT_lo_done, base(phase) + CH)
                for g in range(NG):
                    u = u0 + FFN_UNITS - NG + g
                    s = sums_before(phase) + 2 * NG * (CH - 1) + 2 * g
                    rows_sum(u, u % SPLIT, 1, s, [sums[:, (2 * g) % 4, :], sums[:, (2 * g + 1) % 4, :]])
                    if phase == "ffn1" and g:
                        norm_transposes(1, g - 1)

            def use(name):
                if WORK.index(name):
                    pe.wait_ge(work_free, WORK.index(name))

            def head_transposes(name, of_buffer, n):
                use("T " + name)
                pe.wait_ge(rows_ready, up_to(ROWS, name))
                at = lambda i: work[:, i * P:(i + 1) * P]
                of = lambda i: rows[:, of_buffer, ((i % 2) * n + i // 2) * P:((i % 2) * n + i // 2 + 1) * P]
                transpose(at, of, n * NTOK).then_inc(work_ready, 1)

            def scores1(a):
                use(f"S1 a{a}")
                for h in range(HEADS):
                    last = pe.matmul(work[:, h * SEQ:(h + 1) * SEQ], qT[:, h, P:SEQ], kaT[:, a, :],
                                     start=True, stop=True)
                last.then_inc(work_ready, 1)

            def scores0(a):
                use(f"S0 a{a}")
                for h in range(HEADS):
                    last = pe.matmul(work[:, h * P:(h + 1) * P], qT[:, h, 0:P], kaT[:, a, 0:P],
                                     start=True, stop=True)
                last.then_inc(work_ready, 1)

            def attend(a):
                use(f"PV a{a}")
                pe.wait_ge(v_copied, 1)
                cols = slice(a * HD, (a + 1) * HD)
                for h in range(HEADS):
                    pe.matmul(work[:, h * SEQ:h * SEQ + P], va[:, 0, cols], t0[:, h, :], start=True, stop=True)
                    pe.matmul(work[:, h * SEQ + P:(h + 1) * SEQ], va[:, 0, cols], t1[:, 2 * h, :],
                              start=True, stop=False)
                    last = pe.matmul(work[:, h * SEQ + P:(h + 1) * SEQ], va[:, 1, cols], t1[:, 2 * h + 1, :],
                                     start=False, stop=True)
                last.then_inc(work_ready, 1)

            def retain1(r):
                use(f"R1 r{r}")
                for h in range(HEADS):
                    last = pe.matmul(work[:, h * SEQ:(h + 1) * SEQ], krT[:, h, 0:P], qT[:, h, :],
                                     start=True, stop=True)
                last.then_inc(work_ready, 1)

            def retain0(r):
                use(f"R0 r{r}")
                for h in range(HEADS):
                    last = pe.matmul(work[:, h * P:(h + 1) * P], krT[:, h, P:SEQ], qT[:, h, P:SEQ],
                                     start=True, stop=True)
                last.then_inc(work_ready, 1)

            def retention_rows(r):
                use(f"Y r{r}")
                pe.wait_ge(z_free_s, up_to(Z_SCALAR, f"vr{r}"))
                for h in range(HEADS):
                    cols = slice(h * HD, (h + 1) * HD)
                    pe.matmul(work[:, h * HD:(h + 1) * HD], t1[:, 2 * h, :], vr[:, 0, cols], start=True, stop=True)
                    y1 = work[:, UW + h * HD:UW + (h + 1) * HD]
                    pe.matmul(y1, t1[:, 2 * h + 1, :], vr[:, 0, cols], start=True, stop=False)
                    last = pe.matmul(y1, t0[:, h, :], vr[:, 1, cols], start=False, stop=True)
                last.then_inc(work_ready, 1)

            def side(what):
                kind, _, name = what.partition(" ")
                if kind == "T":
                    head_transposes(name, {"qr0": 1, "kr1": 1}.get(name, 0), 2 if name == "ka" else HEADS)
                elif kind == "TY":
                    use(what)
                    pe.wait_ge(rows_ready, up_to(ROWS, "y " + name))
                    buf = {"r0": 1, "r1": 0}[name]
                    transpose(lambda i: work[:, i * P:(i + 1) * P],
                              lambda i: rows[:, buf, ((i % 2) * KT + i // 2) * P:((i % 2) * KT + i // 2 + 1) * P],
                              KT * NTOK).then_inc(work_ready, 1)
                elif kind == "S1":
                    scores1(int(name[1]))
                elif kind == "S0":
                    scores0(int(name[1]))
                elif kind == "PT1":
                    use(what)
                    pe.wait_ge(rows_ready, up_to(ROWS, "P1 " + name))
                    transpose(lambda i: work[:, i * P:(i + 1) * P],
                              lambda i: s1[:, i // 2, (i % 2) * P:(i % 2 + 1) * P], 2 * HEADS).then_inc(work_ready, 1)
                elif kind == "PT0":
                    use(what)
                    pe.wait_ge(rows_ready, up_to(ROWS, "P0 " + name))
                    transpose(lambda i: work[:, i * P:(i + 1) * P], lambda i: s0[:, i, :],
                              HEADS).then_inc(work_ready, 1)
                elif kind == "PV":
                    attend(int(name[1]))
                elif kind == "R1":
                    retain1(int(name[1]))
                elif kind == "R0":
                    retain0(int(name[1]))
                elif kind == "Y":
                    retention_rows(int(name[1]))

            def pair_free(s):
                if s < 2:
                    return
                kind, name, _ = MIX[s - 2]
                if kind == "out":
                    pe.wait_ge(sum_room, 4 + sums_before("mix") + 2 * NG * OUTS.index(name) + 6)
                elif name in Z_VECTOR:
                    pe.wait_ge(z_free_v, up_to(Z_VECTOR, name))
                else:
                    pe.wait_ge(z_free_s, up_to(Z_SCALAR, name))

            def multiply_mixer():
                u0 = FIRST["mix"]
                pe.wait_ge(silu_done, CH)
                for s, (kind, name, _) in enumerate(MIX):
                    pair_free(s)
                    if s == 0:
                        first_chunk(1, u0)
                    if kind == "out":
                        pe.wait_ge(work_free, up_to(WORK, {"a": "PV ", "r": "TY "}[name[0]] + name))
                    for g in range(4):
                        t = 4 * s + g
                        u = u0 + t
                        if kind == "in":
                            if s:
                                columns(u, u % SPLIT, g, pair[s % 2])
                        else:
                            two = pair[s % 2] if g % 2 == 0 else sums[:, 0:2, :]
                            rows_sum(u, u % SPLIT, {"a0": 0, "a1": 1, "r0": 0, "r1": 1}[name],
                                     sums_before("mix") + 2 * NG * OUTS.index(name) + 2 * g,
                                     [two[:, 0, :], two[:, 1, :]])
                            if name == "r1" and g:
                                if g == 1:
                                    pe.wait_ge(sum_room, 4 + sums_before("mix") + 2 * NG * OUTS.index("r0") + 6)
                                norm_transposes(2, g - 1)
                        for what in AFTER.get(t, ()):
                            side(what)

            multiply_ffn("ffn1", 0)
            multiply_mixer()
            multiply_ffn("ffn2", 2)

        @block.scalar
        def _(act):
            def split_hi(u, slot, raw_slot, loads):
                act.wait_ge(raw_landed[raw_slot], 16 * loads)
                act.wait_ge(unit_done, u - SPLIT + 1)
                act.activation(w_hi[:, slot, :, :], raw[:, raw_slot, :, :], ACT.Copy).then_inc(hi_done, 1)

            def split(u):
                if u < UNITS:
                    if u < SPLIT:
                        act.wait_ge(raw_landed[u % RAW], 16)
                        act.activation(w_hi[:, u, :, :], raw[:, u, :, :], ACT.Copy).then_inc(hi_done, 1)
                    else:
                        split_hi(u, u % SPLIT, u % RAW, u // RAW + 1)

            def square_x(n, g):
                if n:
                    act.wait_ge(sum_room, 4 + sums_before(["", "mix", "ffn2"][n]) - 2 * (NG - 1 - g))
                for t in range(NTOK):
                    if n or g or t:
                        act.wait_ge(squared, (n * NG + g) * NTOK + t)
                    act.activation(square[:, 0:UW], xs[:, t, g * UW:(g + 1) * UW], ACT.Square,
                                   accum_out=ssq[:, t, g:g + 1]).then_inc(squared, 1)

            def split_first(g):
                act.wait_ge(gcol_landed, 16)
                act.wait_ge(xT_landed[g], 16)
                for k in range(KT):
                    cols = slice(k * SEQ, (k + 1) * SEQ)
                    last = act.activation(hT_hi[:, g, cols], rows[:, g % 2, cols], ACT.Copy,
                                          scale=gcol[:, g * KT + k:g * KT + k + 1])
                last.then_inc(hT_hi_done, 1)

            def split_norm(n, g):
                act.wait_ge(hT_raw, (n - 1) * KG + g + 1)
                act.activation(hT_hi[:, g, :], flat(pair[1]), ACT.Copy).then_inc(hT_hi_done, 1)

            def root_x(n):
                act.wait_ge(mean_ready, n + 1)
                act.activation(nst[:, 4:6], nst[:, 2:4], ACT.Sqrt).then_inc(root_ready, 1)

            def after_norm_unit(n, g):
                if g:
                    split_norm(n, g - 1)
                square_x(n, g)

            def after_first_unit(n, g):
                if n and g == 1:
                    split_norm(n, KG - 1)
                    root_x(n)

            def split_activation(phase, c, which=0):
                act.wait_ge(aT_raw, base(phase) + c + 1)
                act.activation(aT_hi[:, which, :], flat(pair[1]), ACT.Copy).then_inc(aT_hi_done, 1)

            def scaled(to, z, func, cols=UW):
                for t in range(NTOK):
                    last = act.activation(to[:, t * cols:(t + 1) * cols], z[:, t, :], func, scale=rms[:, t:t + 1])
                return last

            def silu(phase, c, u, used=True):
                act.wait_ge(unit_done, u + 1)
                if used:
                    act.wait_ge(act_ready, base(phase) + c)
                scaled(gate_s[:, :], pair[0], ACT.Silu).then_inc(silu_done, 1)

            def ffn_side(phase):
                u0, n = FIRST[phase], 0 if phase == "ffn1" else 2
                for i in range(2 * KG):
                    if u0 + i + LEAD >= EARLY:
                        split(u0 + i + LEAD)
                    if i < KG:
                        after_first_unit(n, i)
                    if i == KG - 1:
                        act.wait_ge(rms_ready, n + 1)
                        silu(phase, 0, u0 + i, used=phase == "ffn2")

                def chunk(c, last=False):
                    u = u0 + 2 * KG + (c - 1) * 12
                    for j in range(12):
                        i = 2 * KG + j + LEAD
                        split_hi(u + j + LEAD, i % SPLIT, i % RAW, (c - 1) * (12 // RAW) + (u0 + i) // RAW + 1)
                        if j == 1:
                            split_activation(phase, c - 1)
                        if j == KG - 1:
                            silu(phase, c, u + j)
                        if last and j == 2 * KG + 1:
                            split_activation(phase, c, 1)

                with act.Fori(1, CH - 1) as c:
                    chunk(c)
                chunk(CH - 1, last=True)
                for g in range(NG):
                    split(u0 + FFN_UNITS - NG + g + LEAD)
                    if phase == "ffn1":
                        after_norm_unit(1, g)

            def z_done(name):
                act.wait_ge(unit_done, FIRST["mix"] + 4 * CHUNK_OF[name] + 4)

            def wait_work(name):
                act.wait_ge(work_ready, up_to(WORK, name))

            def root(name, n=NTOK * HEADS):
                act.wait_ge(head_mean, up_to(STATS, name))
                act.activation(hst[:, 2, 0:n], hst[:, 1, 0:n], ACT.Sqrt).then_inc(head_root, 1)

            def exps(k, a, s, width):
                act.wait_ge(score_max, k)
                for h in range(HEADS):
                    act.activation(s[:, h, :], s[:, h, :], ACT.Exp, bias=sst[:, 2, h:h + 1],
                                   accum_out=sst[:, 4, h:h + 1])
                act.activation(sst[:, 5, :], sst[:, 3, :], ACT.Exp).then_inc(exp_done, 1)

            def copy_work(name, to, n):
                wait_work(name)
                act.activation(to, work[:, 0:n], ACT.Copy).then_inc(work_free, 1)

            def side(what):
                kind, _, name = what.partition(" ")
                if what == "ka":
                    z_done("kv")
                    z = pair[CHUNK_OF["kv"] % 2]
                    act.wait_ge(rms_ready, 2)
                    act.wait_ge(squared, 2 * NG * NTOK)
                    scaled(va[:, :, :].rearrange("p t n -> p (t n)"), z[:, :, 2 * HD:4 * HD], ACT.Copy,
                           2 * HD).then_inc(v_copied, 1)
                    scaled(square[:, 0:4 * HD], z[:, :, 0:2 * HD], ACT.Square, 2 * HD).then_inc(head_sq, 1)
                    root("ka", 4)
                elif what in ("qa0", "qa1"):
                    z_done(what)
                    scaled(square[:, :], pair[CHUNK_OF[what] % 2], ACT.Square).then_inc(head_sq, 1)
                    root(what)
                elif kind == "T":
                    to = {"ka": kaT, "kr0": krT, "kr1": krT}.get(name, qT)
                    copy_work(what, to[:, :, :].rearrange("p h n -> p (h n)"), 2 * SEQ if name == "ka" else HEADS * SEQ)
                elif kind == "S1":
                    exps(2 * int(name[1]) + 1, int(name[1]), s1, SEQ)
                elif kind == "S0":
                    exps(2 * int(name[1]) + 2, int(name[1]), s0, P)
                elif kind == "PT1":
                    copy_work(what, t1[:, :, :].rearrange("p h n -> p (h n)"), 2 * HEADS * P)
                elif kind == "PT0":
                    copy_work(what, t0[:, :, :].rearrange("p h n -> p (h n)"), HEADS * P)
                elif kind in ("PV", "TY"):
                    wait_work(what)
                    act.activation(aT_hi[:, int(name[1]), :], work, ACT.Copy).then_inc(mT_hi_done, 1)
                elif what in ("vr0", "vr1"):
                    z_done(what)
                    if what == "vr1":
                        wait_work("Y r0")
                    scaled(vr[:, :, :].rearrange("p t n -> p (t n)"), pair[CHUNK_OF[what] % 2],
                           ACT.Copy).then_inc(z_free_s, 1)
                elif kind == "Y":
                    wait_work(what)
                    act.activation(square[:, :], work, ACT.Square).then_inc(head_sq, 1)
                    root("y " + name)
                elif what in ("gr0", "gr1"):
                    z_done(what)
                    if what == "gr0":
                        act.wait_ge(act_ready, CH)
                    else:
                        act.wait_ge(rows_ready, up_to(ROWS, "y r0"))
                    scaled(gate_s[:, :], pair[CHUNK_OF[what] % 2], ACT.Silu).then_inc(z_free_s, 1)

            def mixer_side():
                for t in range(MIX_UNITS):
                    split(FIRST["mix"] + t + LEAD)
                    for what in AFTER.get(t, ()):
                        side(what)
                    if t < KG:
                        after_first_unit(1, t)
                    if t // 4 == CHUNK_OF["r1"]:
                        after_norm_unit(2, t % 4)

            for g in range(KG):
                split(g)
                split_first(g)
            for u in range(KG, EARLY):
                split(u)
            for g in range(NG):
                act.wait_ge(x_landed[g], 16)
                square_x(0, g)
            root_x(0)
            ffn_side("ffn1")
            mixer_side()
            ffn_side("ffn2")

        @block.vector
        def _(dve):
            links = [0]

            def mark(ins):
                links[0] += 1
                ins.then_inc(chain, 1)

            def settle():
                dve.wait_ge(chain, links[0])

            def split_lo(u, slot, raw_slot):
                dve.wait_ge(hi_done, u + 1)
                dve.tensor_tensor(w_lo[:, slot, :, :], raw[:, raw_slot, :, :], w_hi[:, slot, :, :].bitcast(F32),
                                  ALU.subtract).then_inc(lo_done, 1)

            def split(u):
                if u < UNITS:
                    split_lo(u, u % SPLIT, u % RAW)

            def apply_gain(n, g):
                dve.wait_ge(gain_landed[g], 16 * n)
                if g >= 2:
                    dve.wait_ge(hT_raw, (n - 1) * KG + g - 1)
                dve.wait_ge(sum_room, 4 + sums_before(["", "mix", "ffn2"][n]) - 2 * (NG - 1 - g))
                cols = slice(g * UW, (g + 1) * UW)
                dve.tensor_tensor(rows[:, g % 2, :].rearrange("p (t n) -> p t n", t=NTOK), xs[:, :, cols],
                                  table[:, cols].unsqueeze(1).to_broadcast([P, NTOK, UW]),
                                  ALU.mult).then_inc(gained, 1)

            def low_first(g):
                dve.wait_ge(hT_hi_done, g + 1)
                for k in range(KT):
                    cols = slice(k * SEQ, (k + 1) * SEQ)
                    last = dve.scalar_tensor_tensor(out=hT_lo[:, g, cols], in0=rows[:, g % 2, cols],
                                                    scalar=gcol[:, g * KT + k:g * KT + k + 1],
                                                    in1=hT_hi[:, g, cols].bitcast(F32), op0=ALU.mult,
                                                    op1=ALU.subtract)
                last.then_inc(hT_lo_done, 1)

            def low_norm(n, g):
                dve.wait_ge(hT_hi_done, n * KG + g + 1)
                dve.tensor_tensor(hT_lo[:, g, :], flat(pair[1]), hT_hi[:, g, :].bitcast(F32),
                                  ALU.subtract).then_inc(hT_lo_done, 1)

            def rms_of_x(n):
                dve.wait_ge(squared, NTOK * NG * (n + 1))
                mark(dve.tensor_reduce(nst[:, 0:2], ssq[:, :, :], AX_X, ALU.add))
                settle()
                dve.tensor_scalar(nst[:, 2:4], nst[:, 0:2], 1.0 / D_MODEL, EPS, ALU.mult, ALU.add).then_inc(mean_ready, 1)
                dve.wait_ge(root_ready, n + 1)
                dve.reciprocal(rms, nst[:, 4:6]).then_inc(rms_ready, 1)

            def after_norm_unit(n, g):
                apply_gain(n, g)
                if g:
                    low_norm(n, g - 1)

            def after_first_unit(n, g):
                if n and g == 1:
                    low_norm(n, KG - 1)
                    rms_of_x(n)

            def add_sums(u, earlier, g, to, scale):
                for t in range(NTOK):
                    if t == 0:
                        dve.wait_ge(half_done, earlier + 1)
                    else:
                        dve.wait_ge(unit_done, u + 1)
                    part = xs[:, t, g * UW:(g + 1) * UW]
                    dve.scalar_tensor_tensor(out=part, in0=to[t], scalar=scale, in1=part, op0=ALU.mult,
                                             op1=ALU.add).then_inc(sum_room, 1)

            def split_activation(phase, c, which=0):
                dve.wait_ge(aT_hi_done, base(phase) + c + 1)
                dve.tensor_tensor(aT_lo[:, which, :], flat(pair[1]), aT_hi[:, which, :].bitcast(F32),
                                  ALU.subtract).then_inc(aT_lo_done, 1)

            def multiply_up(phase, c, u):
                dve.wait_ge(unit_done, u + 1)
                dve.wait_ge(silu_done, base(phase) + c + 1)
                for t in range(NTOK):
                    cols = slice(t * UW, (t + 1) * UW)
                    last = dve.scalar_tensor_tensor(out=act_s[:, cols], in0=pair[1][:, t, :], scalar=rms[:, t:t + 1],
                                                    in1=gate_s[:, cols], op0=ALU.mult, op1=ALU.mult)
                last.then_inc(act_ready, 1)

            def ffn_side(phase):
                u0 = FIRST[phase]
                for i in range(2 * KG):
                    if u0 + i + LEAD >= EARLY:
                        split(u0 + i + LEAD)
                    if i < KG:
                        after_first_unit(0 if phase == "ffn1" else 2, i)
                    if i == 2 * KG - 1:
                        multiply_up(phase, 0, u0 + i)

                def chunk(c, last=False):
                    u = u0 + 2 * KG + (c - 1) * 12
                    for j in range(12):
                        i = 2 * KG + j + LEAD
                        split_lo(u + j + LEAD, i % SPLIT, i % RAW)
                        if j == 1:
                            split_activation(phase, c - 1)
                        if j == 2 * KG - 1:
                            multiply_up(phase, c, u + j)
                        if j >= 2 * KG:
                            g = j - 2 * KG
                            add_sums(u + j, sums_before(phase) // 2 + NG * (c - 1) + g, g,
                                     [sums[:, (2 * g) % 4, :], sums[:, (2 * g + 1) % 4, :]], 0.5)
                        if last and j == 2 * KG + 1:
                            split_activation(phase, c, 1)

                with dve.Fori(1, CH - 1) as c:
                    chunk(c)
                chunk(CH - 1, last=True)
                for g in range(NG):
                    u = u0 + FFN_UNITS - NG + g
                    split(u + LEAD)
                    add_sums(u, sums_before(phase) // 2 + NG * (CH - 1) + g, g,
                             [sums[:, (2 * g) % 4, :], sums[:, (2 * g + 1) % 4, :]], 0.5)
                    if phase == "ffn1":
                        after_norm_unit(1, g)

            def wait_work(name):
                dve.wait_ge(work_ready, up_to(WORK, name))

            def own_rows(name):
                if ROWS.index(name):
                    dve.wait_ge(rows_ready, ROWS.index(name))

            def head_stats(name, n):
                dve.wait_ge(head_sq, up_to(STATS, name))
                mark(dve.tensor_reduce(hst[:, 0, 0:n], square[:, 0:n * HD].rearrange("p (h d) -> p h d", d=HD),
                                       AX_X, ALU.add))
                settle()
                dve.tensor_scalar(hst[:, 1, 0:n], hst[:, 0, 0:n], 1.0 / HD, EPS, ALU.mult,
                                  ALU.add).then_inc(head_mean, 1)
                dve.wait_ge(head_root, up_to(STATS, name))
                mark(dve.reciprocal(hst[:, 3, 0:n], hst[:, 2, 0:n]))
                settle()

            def each(a, n, d):
                return a.unsqueeze(2).to_broadcast([P, n, d])

            def norm_heads(name, heads, gain, buf, last_use):
                n = NTOK * heads
                z = pair[CHUNK_OF["kv" if name == "ka" else name] % 2][:, :, 0:heads * HD]
                out_rows = rows[:, buf, 0:n * HD]
                if last_use:
                    wait_work(last_use)
                own_rows(name)
                head_stats(name, n)
                mark(dve.tensor_tensor(hst[:, 0, 0:n].rearrange("p (t h) -> p t h", t=NTOK),
                                       hst[:, 3, 0:n].rearrange("p (t h) -> p t h", t=NTOK),
                                       rms.unsqueeze(2).to_broadcast([P, NTOK, heads]), ALU.mult))
                settle()
                r4 = out_rows.rearrange("p (t h d) -> p t h d", t=NTOK, h=heads)
                dve.tensor_tensor(r4, z.rearrange("p t (h d) -> p t h d", d=HD),
                                  hst[:, 0, 0:n].rearrange("p (t h) -> p t h", t=NTOK).unsqueeze(3)
                                  .to_broadcast([P, NTOK, heads, HD]), ALU.mult).then_inc(z_free_v, 1)
                dve.wait_ge(z_free_v, up_to(Z_VECTOR, "kv" if name == "ka" else name))
                rf = out_rows.rearrange("p (h d) -> p h d", d=HD)
                mark(dve.tensor_tensor(rf, rf, gain[:, :].unsqueeze(1).to_broadcast([P, n, HD]), ALU.mult))
                settle()
                half = ROPE // 2
                turned = act_s[:, 0:n * ROPE].rearrange("p (t h d) -> p t h d", t=NTOK, h=heads)
                over = lambda a, w: a.unsqueeze(2).to_broadcast([P, NTOK, heads, w])
                mark(dve.tensor_tensor(turned[:, :, :, 0:half], r4[:, :, :, half:ROPE],
                                       over(sin_a[:, :, 0:half], half), ALU.mult))
                mark(dve.tensor_tensor(turned[:, :, :, half:ROPE], r4[:, :, :, 0:half],
                                       over(sin_a[:, :, half:ROPE], half), ALU.mult))
                settle()
                mark(dve.tensor_tensor(r4[:, :, :, 0:ROPE], r4[:, :, :, 0:ROPE], over(cos_a, ROPE), ALU.mult))
                settle()
                dve.tensor_tensor(r4[:, :, :, 0:ROPE], r4[:, :, :, 0:ROPE], turned, ALU.add).then_inc(rows_ready, 1)

            def rotate_heads(name, buf, last_use):
                z = pair[CHUNK_OF[name] % 2].rearrange("p t (h d) -> p t h d", d=HD)
                dve.wait_ge(unit_done, FIRST["mix"] + 4 * CHUNK_OF[name] + 4)
                own_rows(name)
                if last_use:
                    wait_work(last_use)
                half = HD // 2
                r4 = rows[:, buf, :].rearrange("p (t h d) -> p t h d", t=NTOK, h=HEADS)
                turned = act_s[:, :].rearrange("p (t h d) -> p t h d", t=NTOK, h=HEADS)
                over = lambda a, w: a.unsqueeze(2).to_broadcast([P, NTOK, HEADS, w])
                mark(dve.tensor_tensor(r4, z, over(cos_r, HD), ALU.mult))
                mark(dve.tensor_tensor(turned[:, :, :, 0:half], z[:, :, :, half:HD],
                                       over(sin_r[:, :, 0:half], half), ALU.mult))
                dve.tensor_tensor(turned[:, :, :, half:HD], z[:, :, :, 0:half],
                                  over(sin_r[:, :, half:HD], half), ALU.mult).then_inc(z_free_v, 1)
                settle()
                dve.wait_ge(z_free_v, up_to(Z_VECTOR, name))
                dve.tensor_tensor(r4, r4, turned, ALU.add).then_inc(rows_ready, 1)

            def softmax(what, k, a, s, width, masked):
                wait_work(what)
                own_rows(what.replace("S", "P"))
                dve.scalar_tensor_tensor(out=s[:, :, :], in0=work[:, 0:HEADS * width].rearrange("p (h n) -> p h n", n=width),
                                         scalar=float(HD) ** -0.5,
                                         in1=masked.unsqueeze(1).to_broadcast([P, HEADS, width]),
                                         op0=ALU.mult, op1=ALU.add).then_inc(work_free, 1)
                dve.wait_ge(work_free, up_to(WORK, what))
                mark(dve.tensor_reduce(sst[:, 0, :], s[:, :, :], AX_X, ALU.max))
                settle()
                sinks4 = sink[:, a * HEADS:(a + 1) * HEADS]
                mark(dve.tensor_tensor(sst[:, 1, :], sst[:, 0, :], sinks4, ALU.max))
                settle()
                mark(dve.tensor_scalar(sst[:, 2, :], sst[:, 1, :], -1.0, None, ALU.mult))
                dve.tensor_tensor(sst[:, 3, :], sinks4, sst[:, 1, :], ALU.subtract).then_inc(score_max, 1)
                dve.wait_ge(exp_done, k)
                mark(dve.tensor_tensor(sst[:, 6, :], sst[:, 4, :], sst[:, 5, :], ALU.add))
                settle()
                mark(dve.reciprocal(sst[:, 7, :], sst[:, 6, :]))
                settle()
                dve.tensor_tensor(s[:, :, :], s[:, :, :], each(sst[:, 7, :], HEADS, width),
                                  ALU.mult).then_inc(rows_ready, 1)

            def decayed(what, r, to, width):
                wait_work(what)
                dve.wait_ge(decay_landed, 16)
                dve.tensor_tensor(to[:, :, :].rearrange("p a n -> p (a n)").rearrange("p (h n) -> p h n", h=HEADS),
                                  work[:, 0:HEADS * width].rearrange("p (h n) -> p h n", n=width),
                                  decays[:, r * HEADS:(r + 1) * HEADS, 0:width], ALU.mult).then_inc(work_free, 1)

            def side(what):
                kind, _, name = what.partition(" ")
                if what == "ka":
                    dve.wait_ge(const_landed, 64)
                    dve.wait_ge(rms_ready, 2)
                    for t in range(NTOK):
                        mark(dve.tensor_scalar(turn[:, t, :, :], turn[:, t, :, :], rms[:, t:t + 1], None, ALU.mult))
                    norm_heads("ka", 2, kgain, 0, None)
                elif what == "qa0":
                    norm_heads("qa0", HEADS, qgain, 0, "T ka")
                elif what == "qa1":
                    norm_heads("qa1", HEADS, qgain, 0, "T qa0")
                elif what == "qr0":
                    rotate_heads(what, 1, None)
                elif what == "kr0":
                    rotate_heads(what, 0, "T qa1")
                elif what == "qr1":
                    rotate_heads(what, 0, "T kr0")
                elif what == "kr1":
                    rotate_heads(what, 1, "TY r0")
                elif kind == "S1":
                    a = int(name[1])
                    softmax(what, 2 * a + 1, a, s1, SEQ, mask)
                elif kind == "S0":
                    a = int(name[1])
                    softmax(what, 2 * a + 2, a, s0, P, mask[:, P:SEQ])
                elif kind in ("PV", "TY"):
                    dve.wait_ge(mT_hi_done, up_to(OUTS, name))
                    dve.tensor_tensor(aT_lo[:, int(name[1]), :], work, aT_hi[:, int(name[1]), :].bitcast(F32),
                                      ALU.subtract).then_inc(work_free, 1)
                elif kind == "R1":
                    decayed(what, int(name[1]), t1, SEQ)
                elif kind == "R0":
                    decayed(what, int(name[1]), t0, P)
                elif kind == "Y":
                    buf, last_use = {"r0": (1, "T qr0"), "r1": (0, "T qr1")}[name]
                    wait_work(last_use)
                    head_stats("y " + name, NTOK * HEADS)
                    dve.tensor_tensor(rows[:, buf, :].rearrange("p (h d) -> p h d", d=HD),
                                      work.rearrange("p (h d) -> p h d", d=HD),
                                      each(hst[:, 3, :], NTOK * HEADS, HD), ALU.mult).then_inc(work_free, 1)
                elif what in ("gr0", "gr1"):
                    buf = {"gr0": 1, "gr1": 0}[what]
                    dve.wait_ge(z_free_s, up_to(Z_SCALAR, what))
                    dve.wait_ge(work_free, up_to(WORK, "Y " + what[1:]))
                    dve.tensor_tensor(rows[:, buf, :], rows[:, buf, :], gate_s[:, :], ALU.mult).then_inc(rows_ready, 1)

            def mixer_side():
                for t in range(MIX_UNITS):
                    split(FIRST["mix"] + t + LEAD)
                    s, g = divmod(t, 4)
                    kind, name, _ = MIX[s]
                    if kind == "out":
                        two = pair[s % 2] if g % 2 == 0 else sums[:, 0:2, :]
                        add_sums(FIRST["mix"] + t, sums_before("mix") // 2 + NG * OUTS.index(name) + g, g,
                                 [two[:, 0, :], two[:, 1, :]], 1.0)
                    if t < KG:
                        after_first_unit(1, t)
                    if name == "r1":
                        after_norm_unit(2, g)
                    for what in AFTER.get(t, ()):
                        side(what)

            for i in range(4):
                dve.memset(spare[:, i:i + 1], 0.0).then_inc(sum_room, 1)
            for g in range(KG):
                split(g)
                low_first(g)
            for u in range(KG, EARLY):
                split(u)
            rms_of_x(0)
            ffn_side("ffn1")
            mixer_side()
            ffn_side("ffn2")


def tables():
    import numpy as np
    f32 = np.float32

    def rotary(dim, theta):
        inv = f32(theta) ** (-np.arange(0, dim, 2, dtype=f32) / f32(dim))
        ang = np.arange(SEQ, dtype=f32)[:, None] * inv[None, :]
        cos, sin = np.cos(ang), np.sin(ang)
        both = np.concatenate([cos, cos], 1), np.concatenate([-sin, sin], 1)
        return [a.reshape(NTOK, P, dim).transpose(1, 0, 2).reshape(P, NTOK * dim) for a in both]

    i, j = np.arange(P)[:, None], np.arange(SEQ)[None, :]
    mask = np.where((j > i) & (j <= P + i), 0.0, NEG)
    cos, sin = (a.reshape(P, NTOK, HD) for a in rotary(HD, 10000.0))
    turn = np.stack([cos, sin], 2).reshape(P, -1)
    const = np.concatenate([np.eye(P), *rotary(ROPE, 500000.0), mask, turn], 1).astype(f32)
    gamma = 1.0 - 2.0 ** (-5.0 - np.arange(2 * HEADS))
    ago = j - i
    decay = np.where(ago >= 0, gamma[:, None, None] ** np.maximum(ago, 0), 0.0) * HD ** -0.5
    return const, np.ascontiguousarray(decay.transpose(1, 0, 2).reshape(P, -1).astype(f32))


def by_units(w, down):
    import numpy as np
    k, n = w.shape[1:]
    tiles = w[0].reshape(k // UW, KT, P, n // UW, UW)
    tiles = tiles.transpose(0, 3, 2, 1, 4) if down else tiles.transpose(3, 0, 2, 1, 4)
    return np.ascontiguousarray(tiles).reshape(*tiles.shape[:2], P, KT * UW)


_INS = ["x", "mix_norm", "ffn2_norm", "q_norm", "k_norm", "attn_sinks"]
_FIRST = ["ffn1_w_gate", "ffn1_w_up", "ffn2_w_gate", "ffn2_w_up", "w_in"]
_SECOND = ["ffn1_w_down", "ffn2_w_down", "w_out"]


def kernel(**inputs):
    import numpy as np
    import concourse.bacc as bacc
    from concourse.bass_utils import run_bass_kernel_spmd

    const, decay = tables()
    arrays = {name: np.ascontiguousarray(inputs[name]) for name in _INS}
    arrays["consts"], arrays["decays"] = const, decay
    arrays |= {name: by_units(np.asarray(inputs[name]), name in _SECOND) for name in _FIRST + _SECOND}
    arrays["xT"] = np.ascontiguousarray(arrays["x"][0].T.reshape(KG, KT, P, SEQ).transpose(0, 2, 1, 3)).reshape(
        KG, P, KT * SEQ)
    arrays["ffn1_gain"] = np.ascontiguousarray(np.asarray(inputs["ffn1_norm"]).reshape(-1, P).T)
    nc = bacc.Bacc("TRN2", target_bir_lowering=False, num_devices=1)
    d = {name: nc.dram_tensor(f"in_{name}", a.shape, mybir.dt.from_np(a.dtype), kind="ExternalInput").ap()
         for name, a in arrays.items()}
    out = nc.dram_tensor("out_x", (1, SEQ, D_MODEL), F32, kind="ExternalOutput").ap()
    build(nc, d["x"], d["xT"], d["ffn1_gain"], [d["mix_norm"], d["ffn2_norm"]],
          {f: (d[f + "_w_gate"], d[f + "_w_up"], d[f + "_w_down"]) for f in ("ffn1", "ffn2")},
          d["w_in"], d["w_out"], d["q_norm"], d["k_norm"], d["attn_sinks"], d["consts"], d["decays"], out)
    r = run_bass_kernel_spmd(nc, [{f"in_{name}": a for name, a in arrays.items()}], core_ids=[0])
    return r.results[0]["out_x"]
```
